# Optimizing a Trainium2 kernel written in Bass

```python
import math
import jax, jax.numpy as jnp
from jax import lax
import numpy as np

D_MODEL = 1024
BATCH = 1
SEQ = 256
DEPTH = 2

HEAD_DIM = 64
N_RET_HEADS = 8
N_MOBA_HEADS = 8
RET_WIDTH = N_RET_HEADS * HEAD_DIM
MOBA_WIDTH = N_MOBA_HEADS * HEAD_DIM
RET_CHUNK = 128
MOBA_BLOCK = 256
MOBA_TOPK = 3
MOBA_Q_BLOCK = 64
GMLP_CHUNK = 128
GMLP_GROUPS = 8
GMLP_WIDTH = 2 * D_MODEL
FFN_HIDDEN = 4 * D_MODEL
ROPE_THETA = 10000.0
LN_EPS = 1e-5
N_EVEN = (DEPTH + 1) // 2
N_ODD = DEPTH // 2
DEEPNORM_ALPHA = (2 * DEPTH) ** 0.25
DEEPNORM_BETA = (8 * DEPTH) ** -0.25
IN_COLS = 4 * RET_WIDTH + 3 * MOBA_WIDTH
IN_SPLITS = [RET_WIDTH * i for i in range(1, 5)] + [4 * RET_WIDTH + MOBA_WIDTH * i for i in range(1, 3)]

kernel_name = "retnet_moba_gmlp_deepnorm_hybrid"

def layer_norm(x, g, b):
    xf = x.astype(jnp.float32)
    mu = jnp.mean(xf, -1, keepdims=True)
    var = jnp.mean(jnp.square(xf - mu), -1, keepdims=True)
    return ((xf - mu) * lax.rsqrt(var + LN_EPS) * g.astype(jnp.float32) + b.astype(jnp.float32)).astype(x.dtype)

def rope_tables(positions):
    inv_freq = ROPE_THETA ** (-jnp.arange(0, HEAD_DIM, 2, dtype=jnp.float32) / HEAD_DIM)
    ang = positions.astype(jnp.float32)[..., None] * inv_freq
    return jnp.cos(ang)[:, None], jnp.sin(ang)[:, None]

def apply_rope(t, cos, sin):
    half = HEAD_DIM // 2
    t1, t2 = t[..., :half], t[..., half:]
    return jnp.concatenate([t1 * cos - t2 * sin, t2 * cos + t1 * sin], -1).astype(t.dtype)

def split_heads(t, n_heads):
    b, s, _ = t.shape
    return t.reshape(b, s, n_heads, HEAD_DIM).transpose(0, 2, 1, 3)

def merge_heads(t):
    b, h, s, d = t.shape
    return t.transpose(0, 2, 1, 3).reshape(b, s, h * d)

def retention(q, k, v):
    b, h, s, d = q.shape
    n = s // RET_CHUNK
    dt = q.dtype
    log_gamma = jnp.log1p(-jnp.exp2(-5.0 - jnp.arange(h, dtype=jnp.float32)))
    idx = jnp.arange(RET_CHUNK, dtype=jnp.float32)
    diff = idx[:, None] - idx[None, :]
    decay = jnp.where(diff >= 0, jnp.exp(log_gamma[:, None, None] * jnp.maximum(diff, 0.0)), 0.0)
    xi = jnp.exp(log_gamma[:, None] * (idx + 1.0))
    zeta = jnp.exp(log_gamma[:, None] * (RET_CHUNK - 1.0 - idx))
    chunk_decay = jnp.exp(log_gamma * RET_CHUNK)
    qc = q.reshape(b, h, n, RET_CHUNK, d)
    kc = k.reshape(b, h, n, RET_CHUNK, d) * (d ** -0.5)
    vc = v.reshape(b, h, n, RET_CHUNK, d)
    scores = jnp.einsum('bhnid,bhnjd->bhnij', qc, kc) * decay[:, None].astype(dt)
    inner = jnp.einsum('bhnij,bhnjd->bhnid', scores, vc)
    kv = jnp.einsum('bhnjd,bhnje->nbhde', kc * zeta[:, None, :, None].astype(dt), vc).astype(jnp.float32)

    def step(state, kv_n):
        return state * chunk_decay[:, None, None] + kv_n, state

    _, states = lax.scan(step, jnp.zeros((b, h, d, d), jnp.float32), kv)
    cross = jnp.einsum('bhnid,nbhde->bhnie', qc, states.astype(dt)) * xi[:, None, :, None].astype(dt)
    return (inner + cross).reshape(b, h, s, d)

def moba_attention(q, k, v):
    b, h, s, d = q.shape
    nb = s // MOBA_BLOCK
    nq = s // MOBA_Q_BLOCK
    topk = min(MOBA_TOPK, nb)
    scale = d ** -0.5
    k_blocks = k.reshape(b, h, nb, MOBA_BLOCK, d)
    v_blocks = v.reshape(b, h, nb, MOBA_BLOCK, d)
    k_mean = jnp.mean(k_blocks.astype(jnp.float32), axis=3)
    q_chunks = jnp.moveaxis(q.reshape(b, h, nq, MOBA_Q_BLOCK, d), 2, 0)
    bi = jnp.arange(b)[:, None, None, None]
    hi = jnp.arange(h)[None, :, None, None]
    blk_ids = jnp.arange(nb)
    q_off = jnp.arange(MOBA_Q_BLOCK)
    k_off = jnp.arange(MOBA_BLOCK)
    n_sel = topk * MOBA_BLOCK

    def one_chunk(args):
        qc, ci = args
        q_start = ci * MOBA_Q_BLOCK
        own = q_start // MOBA_BLOCK
        gate = jnp.einsum('bhqd,bhnd->bhqn', qc.astype(jnp.float32), k_mean)
        gate = jnp.where(blk_ids < own, gate, -jnp.inf)
        _, sel = lax.top_k(gate, topk)
        sel_valid = sel < own
        k_sel = k_blocks[bi, hi, sel]
        v_sel = v_blocks[bi, hi, sel]
        s_sel = jnp.einsum('bhqd,bhqkjd->bhqkj', qc, k_sel).astype(jnp.float32) * scale
        s_sel = jnp.where(sel_valid[..., None], s_sel, -jnp.inf).reshape(b, h, MOBA_Q_BLOCK, n_sel)
        k_own = lax.dynamic_index_in_dim(k_blocks, own, axis=2, keepdims=False)
        v_own = lax.dynamic_index_in_dim(v_blocks, own, axis=2, keepdims=False)
        s_own = jnp.einsum('bhqd,bhjd->bhqj', qc, k_own).astype(jnp.float32) * scale
        causal = (own * MOBA_BLOCK + k_off)[None, :] <= (q_start + q_off)[:, None]
        s_own = jnp.where(causal, s_own, -jnp.inf)
        p = jax.nn.softmax(jnp.concatenate([s_sel, s_own], -1), axis=-1).astype(qc.dtype)
        p_sel = p[..., :n_sel].reshape(b, h, MOBA_Q_BLOCK, topk, MOBA_BLOCK)
        return (jnp.einsum('bhqkj,bhqkjd->bhqd', p_sel, v_sel)
                + jnp.einsum('bhqj,bhjd->bhqd', p[..., n_sel:], v_own))

    out = lax.map(one_chunk, (q_chunks, jnp.arange(nq)))
    return jnp.moveaxis(out, 0, 2).reshape(b, h, s, d)

def retention_moba_mixer(x, cos, sin, w_in, gn_gain, w_out):
    proj = x @ w_in
    qa, ka, va, ga, qb, kb, vb = jnp.split(proj, IN_SPLITS, axis=-1)
    ya = retention(apply_rope(split_heads(qa, N_RET_HEADS), cos, sin),
                   apply_rope(split_heads(ka, N_RET_HEADS), cos, sin),
                   split_heads(va, N_RET_HEADS))
    yf = ya.astype(jnp.float32)
    mu = jnp.mean(yf, -1, keepdims=True)
    var = jnp.mean(jnp.square(yf - mu), -1, keepdims=True)
    ya = merge_heads(((yf - mu) * lax.rsqrt(var + LN_EPS)).astype(x.dtype)) * gn_gain
    ya = ya * jax.nn.silu(ga)
    yb = merge_heads(moba_attention(apply_rope(split_heads(qb, N_MOBA_HEADS), cos, sin),
                                    apply_rope(split_heads(kb, N_MOBA_HEADS), cos, sin),
                                    split_heads(vb, N_MOBA_HEADS)))
    return jnp.concatenate([ya, yb], axis=-1) @ w_out

def gmlp_mixer(x, w_uv, b_uv, ln_g, ln_b, w_s, b_s, w_out):
    b, s, _ = x.shape
    hdn = jax.nn.gelu(x @ w_uv + b_uv)
    u, v = jnp.split(hdn, 2, axis=-1)
    v = layer_norm(v, ln_g, ln_b)
    n = s // GMLP_CHUNK
    v = v.reshape(b, n, GMLP_CHUNK, GMLP_GROUPS, GMLP_WIDTH // GMLP_GROUPS)
    causal = jnp.tril(jnp.ones((GMLP_CHUNK, GMLP_CHUNK), dtype=bool))
    ws = jnp.where(causal, w_s, jnp.zeros_like(w_s))
    v = jnp.einsum('gij,bnjgc->bnigc', ws, v) + b_s.T[:, :, None]
    return (u * v.reshape(b, s, GMLP_WIDTH)) @ w_out

def channel_mixer(x, w1, w2):
    return jnp.square(jax.nn.relu(x @ w1)) @ w2

def setup_inputs(seed: int = 0) -> dict:
    key = jax.random.key(seed)
    ks = jax.random.split(key, 18)
    f32 = jnp.float32
    nrm = lambda k, shape, scale: jax.random.normal(k, shape, f32) * scale
    x = jax.random.normal(ks[0], (BATCH, SEQ, D_MODEL), f32)
    offset = jax.random.randint(ks[1], (BATCH, 1), 0, 4096, dtype=jnp.int32)
    positions = offset + jnp.arange(SEQ, dtype=jnp.int32)[None, :]
    return {
        "x": x,
        "positions": positions,
        "ln_gain": 1.0 + nrm(ks[2], (DEPTH, 2, D_MODEL), 0.02),
        "ln_bias": nrm(ks[3], (DEPTH, 2, D_MODEL), 0.02),
        "mix_w_in": nrm(ks[4], (N_EVEN, D_MODEL, IN_COLS), D_MODEL ** -0.5),
        "ret_gn_gain": 1.0 + nrm(ks[5], (N_EVEN, RET_WIDTH), 0.02),
        "mix_w_out": nrm(ks[6], (N_EVEN, RET_WIDTH + MOBA_WIDTH, D_MODEL), (RET_WIDTH + MOBA_WIDTH) ** -0.5 * DEEPNORM_BETA),
        "gmlp_w_uv": nrm(ks[7], (N_ODD, D_MODEL, 2 * GMLP_WIDTH), D_MODEL ** -0.5),
        "gmlp_b_uv": nrm(ks[8], (N_ODD, 2 * GMLP_WIDTH), 0.02),
        "gmlp_ln_gain": 1.0 + nrm(ks[9], (N_ODD, GMLP_WIDTH), 0.02),
        "gmlp_ln_bias": nrm(ks[10], (N_ODD, GMLP_WIDTH), 0.02),
        "gmlp_w_s": nrm(ks[11], (N_ODD, GMLP_GROUPS, GMLP_CHUNK, GMLP_CHUNK), GMLP_CHUNK ** -0.5),
        "gmlp_b_s": 1.0 + nrm(ks[12], (N_ODD, GMLP_GROUPS, GMLP_CHUNK), 0.02),
        "gmlp_w_out": nrm(ks[13], (N_ODD, GMLP_WIDTH, D_MODEL), GMLP_WIDTH ** -0.5 * DEEPNORM_BETA),
        "ffn_w_in": nrm(ks[14], (DEPTH, D_MODEL, FFN_HIDDEN), D_MODEL ** -0.5),
        "ffn_w_out": nrm(ks[15], (DEPTH, FFN_HIDDEN, D_MODEL), FFN_HIDDEN ** -0.5 * DEEPNORM_BETA),
    }

def reference(x, positions, ln_gain, ln_bias, mix_w_in, ret_gn_gain, mix_w_out,
              gmlp_w_uv, gmlp_b_uv, gmlp_ln_gain, gmlp_ln_bias, gmlp_w_s, gmlp_b_s,
              gmlp_w_out, ffn_w_in, ffn_w_out):
    cos, sin = rope_tables(positions)
    for layer in range(DEPTH):
        i = layer // 2
        if layer % 2 == 0:
            y = retention_moba_mixer(x, cos, sin, mix_w_in[i], ret_gn_gain[i], mix_w_out[i])
        else:
            y = gmlp_mixer(x, gmlp_w_uv[i], gmlp_b_uv[i], gmlp_ln_gain[i], gmlp_ln_bias[i],
                           gmlp_w_s[i], gmlp_b_s[i], gmlp_w_out[i])
        x = layer_norm(DEEPNORM_ALPHA * x + y, ln_gain[layer, 0], ln_bias[layer, 0])
        y = channel_mixer(x, ffn_w_in[layer], ffn_w_out[layer])
        x = layer_norm(DEEPNORM_ALPHA * x + y, ln_gain[layer, 1], ln_bias[layer, 1])
    return x


_drawn_inputs = setup_inputs


def setup_inputs(seed=0):
    import zlib

    import numpy as np

    out = dict(_drawn_inputs(seed))
    spreads = {}
    factors = {'ret_gn_gain': 23.74,
     'gmlp_b_uv': 8.0,
     'gmlp_ln_gain': 43.006,
     'gmlp_ln_bias': 46.394,
     'gmlp_b_s': 31.0}
    for name, (base, spread) in spreads.items():
        noise = np.random.default_rng([zlib.crc32(name.encode()), seed]).standard_normal(out[name].shape)
        drawn = base * np.exp(spread * noise) if base else spread * noise
        out[name] = __import__('jax').numpy.asarray(drawn.astype(out[name].dtype))
    for name, factor in factors.items():
        out[name] = (out[name] * factor).astype(out[name].dtype)
    return out
```

```python
from contextlib import ExitStack

import numpy as np

import concourse.bass as bass
from concourse import mybir

F32 = mybir.dt.float32
F32R = mybir.dt.float32r
I32 = mybir.dt.int32
ALU = mybir.AluOpType
ACT = mybir.ActivationFunctionType
AX_X = mybir.AxisListType.X

P = 128
SEQ = 256
NT = SEQ // P
D = 1024
KD = D // P
HALF_D = D // 2
HEADS = 8
HD = 64
HEAD_PAIRS = HEADS // 2
ROPE_HALF = HD // 2
RW = HEADS * HD
GROUPS = 8
GW = 2048
GM = GW // P
FF = 4096
FM = FF // P
EPS = 1e-5
ALPHA = float((2 * 2) ** 0.25)
QK_SCALE = float(HD) ** -0.5
MASKED = -3.0e38
LNS = 4

UNIT = 2048
HALF = UNIT // 2
SLOTS = 4
LOOK = 6
N_PROJ, N_OUT, N_FF, N_GV, N_GU, N_GO = 14, 4, 16, 8, 8, 8
U_PROJ = 0
U_OUT = U_PROJ + N_PROJ
U_FA = U_OUT + N_OUT
U_FB = U_FA + N_FF
U_GV = U_FB + N_FF
U_GU = U_GV + N_GV
U_GO = U_GU + N_GU
U_FC = U_GO + N_GO
U_FD = U_FC + N_FF
UNITS = U_FD + N_FF

QB, KB, QA, KA, VB, VA, GA = range(7)
GROUP_COLUMN = [4 * RW, 5 * RW, 0, RW, 6 * RW, 2 * RW, 3 * RW]


def split_bits(value, bits, parts):
    out, rest = [], float(value)
    for n in range(parts):
        if n == parts - 1:
            out.append(float(np.float32(rest)))
        else:
            e = np.floor(np.log2(abs(rest)))
            step = 2.0 ** (e - bits + 1)
            out.append(float(np.trunc(rest / step) * step))
        rest -= out[-1]
        if rest == 0.0:
            break
    return out


class Count:

    def __init__(self, eng, sem):
        self.eng, self.sem, self.n = eng, sem, 0

    def inc(self, ins):
        ins.then_inc(self.sem, 1)
        self.n += 1
        return self.n

    def wait(self, n=None):
        self.eng.wait_ge(self.sem, self.n if n is None else n)


def build(nc, x, positions, ln_gain, ln_bias, mix_w_in, ret_gn_gain, mix_w_out, gmlp_w_uv,
          gmlp_b_uv, gmlp_ln_gain, gmlp_ln_bias, gmlp_w_s, gmlp_b_s, gmlp_w_out, ffn_w_in,
          ffn_w_out, inv_freq, decay, out):
    ctx = ExitStack()
    with ctx:
        def sb(name, shape, dt=F32):
            return ctx.enter_context(nc.sbuf_tensor(name, shape, dt))

        def sem(name):
            return ctx.enter_context(nc.semaphore(name))

        raw = sb("raw", [P, SLOTS, UNIT])
        w_high = sb("w_high", [P, SLOTS, UNIT], F32R)
        w_low = sb("w_low", [P, SLOTS, UNIT], F32R)
        xt_high = sb("xt_high", [P, KD, SEQ], F32R)
        xt_low = sb("xt_low", [P, KD, SEQ], F32R)
        ht_high = sb("ht_high", [P, 4, SEQ], F32R)
        ht_low = sb("ht_low", [P, 4, SEQ], F32R)
        resid = sb("resid", [P, NT, D])
        work = sb("work", [P, NT, D])
        ident = sb("ident", [P, P])
        ones = sb("ones", [P, P])
        small = sb("small", [P, 512])
        arena = sb("arena", [P, 16384])

        def area(start, *shape):
            n = int(np.prod(shape))
            v = arena[:, start:start + n]
            if len(shape) == 2:
                return v.rearrange("p (a b) -> p a b", a=shape[0])
            return v

        qk_t = {g: area(1024 * i, HEAD_PAIRS, SEQ) for i, g in enumerate((QB, KB, QA, KA))}
        qk_n = [area(4096 + 1024 * i, NT, RW) for i in range(2)]
        v_n = {VB: area(6144, NT, RW), VA: area(0, NT, RW)}
        gate = area(1024, NT, RW)
        y_moba, y_ret = qk_n
        p_moba = area(7168, HEADS, 3 * P)
        p_ret = area(10240, HEADS, 3 * P)
        decay_t = area(13312, HEADS, SEQ)
        causal = area(15360, 3 * P)
        gn_gain = area(15744, RW)
        hidden = area(0, FM, SEQ)
        v_gate = area(4096, NT, GW)
        spatial_add = area(8192, GM, P)
        v_bias = area(10240, GW)
        b_s_all = area(10240, GROUPS, P)
        ws_t = area(12288, GROUPS, P)
        ln_tab = area(13312, 2, D)
        ws_n = area(15360, GROUPS, P)

        cos2 = sb("cos2", [P, NT, HD])
        sin2 = sb("sin2", [P, NT, HD])
        ang = sb("ang", [P, NT, ROPE_HALF])
        turns = sb("turns", [P, NT, ROPE_HALF])
        freq = sb("freq", [P, ROPE_HALF])
        pos_i = sb("pos_i", [P, NT], I32)
        rows48 = sb("rows48", [3 * GM, P])
        cols48 = sb("cols48", [P, 3 * GM])
        vn_tile = work[:, 0, 0:512].rearrange("p (s t c) -> p s t c", s=2, t=NT)
        mixed = work[:, 0, 512:1024].rearrange("p (s c) -> p s c", s=2)
        u_tile = work[:, 1, 0:512].rearrange("p (s c) -> p s c", s=2)

        used_cols = [0]

        def cols(n):
            a = used_cols[0]
            used_cols[0] += n
            return small[:, a:a + n]

        pos_f = cols(NT)
        mx = cols(2 * HEADS)
        neg_mx = cols(2 * HEADS)
        p_sum = cols(2 * HEADS)
        p_inv = cols(2 * HEADS)
        gn_stats = cols(6 * 2 * HEADS)
        gn_mv = cols(2 * 2 * HEADS)
        gn_rstd = cols(2 * HEADS)
        ln_stats = cols(6 * 2 * NT)
        ln_mv = cols(2 * NT)
        ln_rstd = cols(NT)
        v_stats = cols(6 * 4 * NT)
        v_mv = cols(2 * NT)
        v_rstd = cols(NT)
        eps_t = cols(2)

        ps_y = ctx.enter_context(nc.psum_tensor("ps_y", [P, 4, 512], F32))
        ps_m = ctx.enter_context(nc.psum_tensor("ps_m", [P, 4, 512], F32))

        raw_landed = [sem(f"raw_landed{i}") for i in range(2 * SLOTS)]
        w_high_ready = sem("w_high_ready")
        w_low_ready = sem("w_low_ready")
        w_used = sem("w_used")
        x_landed = [sem(f"x_landed{t}") for t in range(NT)]
        rope_in_landed = sem("rope_in_landed")
        freq_landed = sem("freq_landed")
        decay_landed = sem("decay_landed")
        gain_landed = sem("gain_landed")
        tab_landed = sem("tab_landed")
        tab2_landed = sem("tab2_landed")
        ws_landed = sem("ws_landed")
        rows_landed = [sem(f"rows_landed{i}") for i in range(3)]
        bs_landed = sem("bs_landed")
        vb_landed = sem("vb_landed")
        out_written = [sem(f"out_written{i}") for i in range(4)]
        consts_ready = sem("consts_ready")
        pool_step = sem("pool_step")
        ones_ready = sem("ones_ready")
        dve_step = sem("dve_step")
        angles_ready = sem("angles_ready")
        rope_tab_ready = sem("rope_tab_ready")
        xt_turned = sem("xt_turned")
        xt_high_ready = sem("xt_high_ready")
        xt_low_ready = sem("xt_low_ready")
        rope_products = sem("rope_products")
        rope_added = sem("rope_added")
        qk_turned = sem("qk_turned")
        qk_t_ready = sem("qk_t_ready")
        moba_scores = sem("moba_scores")
        moba_masked = sem("moba_masked")
        moba_max = sem("moba_max")
        moba_exp = sem("moba_exp")
        p_turned = sem("p_turned")
        p_t_ready = sem("p_t_ready")
        ret_scores = sem("ret_scores")
        ret_decayed = sem("ret_decayed")
        v_ready = sem("v_ready")
        moba_out = sem("moba_out")
        ret_out = sem("ret_out")
        y_moba_ready = sem("y_moba_ready")
        y_ret_ready = sem("y_ret_ready")
        gate_silu = sem("gate_silu")
        gate_ready = sem("gate_ready")
        gn_centred = sem("gn_centred")
        gn_var = sem("gn_var")
        gn_std = sem("gn_std")
        c_turned = sem("c_turned")
        c_high_ready = sem("c_high_ready")
        c_low_ready = sem("c_low_ready")
        y_done = sem("y_done")
        ln_var = sem("ln_var")
        ln_std = sem("ln_std")
        ln_done = sem("ln_done")
        act_out = sem("act_out")
        hidden_ready = sem("hidden_ready")
        ht_high_ready = sem("ht_high_ready")
        ht_low_ready = sem("ht_low_ready")
        ws_masked = sem("ws_masked")
        ws_turned = sem("ws_turned")
        ws_t_ready = sem("ws_t_ready")
        row_sums = sem("row_sums")
        spatial_add_ready = sem("spatial_add_ready")
        v_biased = sem("v_biased")
        v_gelu = sem("v_gelu")
        v_stat = sem("v_stat")
        v_var = sem("v_var")
        v_std = sem("v_std")
        vn_ready = sem("vn_ready")
        spatial_done = sem("spatial_done")
        mixed_ready = sem("mixed_ready")

        x_v = x[0].rearrange("(t p) d -> p t d", p=P)
        out_v = out[0].rearrange("(t p) d -> p t d", p=P)
        w_in_v = mix_w_in[0].rearrange("(k p) n -> p k n", p=P)
        w_out_v = mix_w_out[0].rearrange("(k p) n -> p k n", p=P)
        w_uv_v = gmlp_w_uv[0].rearrange("(k p) n -> p k n", p=P)
        w_go_v = gmlp_w_out[0].rearrange("(k p) n -> p k n", p=P)
        w1_v = [ffn_w_in[l].rearrange("(k p) n -> p k n", p=P) for l in range(2)]
        w2_v = [ffn_w_out[l].rearrange("(k p) n -> p k n", p=P) for l in range(2)]

        def wide(tile, slot):
            return tile[:, slot, :].rearrange("p (k n) -> p k n", k=4)

        def tall(tile, slot, half):
            return tile[:, slot, half * HALF:(half + 1) * HALF].rearrange("p (k c) -> p k c", k=KD)

        def flat(tile, slot, half):
            return tile[:, slot, half * HALF:(half + 1) * HALF]

        def split_high(act, unit_base, j, i=0):
            u, h = unit_base + j // 2, j % 2
            half = 2 * unit_base + j
            act.wait_ge(raw_landed[half % (2 * SLOTS)], 16 * (u // SLOTS + 1 + i))
            if half >= 2 * SLOTS:
                act.wait_ge(w_used, half - 2 * SLOTS + 1 + 8 * i)
            nc.scalar.activation(flat(w_high, u % SLOTS, h), flat(raw, u % SLOTS, h),
                                 ACT.Copy).then_inc(w_high_ready, 1)

        def split_low(dve, unit_base, j, i=0):
            u, h = unit_base + j // 2, j % 2
            dve.wait_ge(w_high_ready, 2 * unit_base + j + 1 + 8 * i)
            nc.vector.tensor_tensor(flat(w_low, u % SLOTS, h), flat(raw, u % SLOTS, h),
                                    flat(w_high, u % SLOTS, h), ALU.subtract).then_inc(w_low_ready, 1)

        total_halves = 2 * UNITS

        def ahead(step, eng, unit_base, j, i=0):
            if 2 * unit_base + j + LOOK < total_halves:
                half = 2 * unit_base + j + LOOK
                step(eng, half // 2, half % 2, i)

        block = ctx.enter_context(nc.Block())

        @block.sync
        def _(sp):
            def load(half, i, src):
                if half >= 2 * SLOTS:
                    sp.wait_ge(w_low_ready, half - 2 * SLOTS + 1 + 8 * i)
                dst = flat(raw, half // 2 % SLOTS, half % 2)
                if len(src.shape) == 3:
                    dst = dst.rearrange("p (k n) -> p k n", k=src.shape[1])
                sp.dma_start(dst, src).then_inc(raw_landed[half % (2 * SLOTS)], 16)

            def load_tall(view, unit_base, n):
                with sp.Fori(0, n // 4) as i:
                    for j in range(8):
                        load(2 * unit_base + j, i, view[:, :, bass.ds((8 * i + j) * P, P)])

            def load_rows(view, unit_base, n):
                with sp.Fori(0, n // 4) as i:
                    for j in range(8):
                        load(2 * unit_base + j, i, view[:, bass.ds(8 * i + j, 1), :])

            def load_tables(ln):
                if ln == 0:
                    sp.wait_ge(ret_decayed, HEADS)
                else:
                    sp.wait_ge(ln_done, 4 * ln)
                sp.dma_start(ln_tab[:, 0, :], ln_gain[ln // 2, ln % 2].partition_broadcast(P)) \
                  .then_inc(tab_landed, 16)
                sp.dma_start(ln_tab[:, 1, :], ln_bias[ln // 2, ln % 2].partition_broadcast(P)) \
                  .then_inc(tab2_landed, 16)

            for t in range(NT):
                sp.dma_start(resid[:, t, :], x_v[:, t, :]).then_inc(x_landed[t], 16)
            for j in range(2 * N_PROJ):
                c = GROUP_COLUMN[j // 4]
                load(j, 0, w_in_v[:, 2 * (j % 4):2 * (j % 4) + 2, c:c + RW])
                if j == 7:
                    sp.dma_start(decay_t, decay.rearrange("p (h i) -> p h i", h=HEADS)) \
                      .then_inc(decay_landed, 16)
                    sp.dma_start(gn_gain, ret_gn_gain[0].partition_broadcast(P)) \
                      .then_inc(gain_landed, 16)
            for j in range(2 * N_OUT):
                k = (4 + j) % KD
                load(2 * U_OUT + j, 0, w_out_v[:, k, :])
            load_tables(0)
            load_tall(w1_v[0], U_FA, N_FF)
            sp.wait_ge(ln_done, 4)
            sp.dma_start(ws_n, gmlp_w_s[0].rearrange("g i j -> i g j")).then_inc(ws_landed, 16)
            sp.dma_start(rows48[0:GM, :], gmlp_b_uv[0, 0:GW].rearrange("(m c) -> m c", m=GM)) \
              .then_inc(rows_landed[0], 16)
            sp.dma_start(rows48[GM:2 * GM, :], gmlp_ln_gain[0].rearrange("(m c) -> m c", m=GM)) \
              .then_inc(rows_landed[1], 16)
            sp.dma_start(rows48[2 * GM:3 * GM, :], gmlp_ln_bias[0].rearrange("(m c) -> m c", m=GM)) \
              .then_inc(rows_landed[2], 16)
            sp.dma_start(b_s_all, gmlp_b_s[0].partition_broadcast(P)).then_inc(bs_landed, 16)
            load_tables(1)
            load_rows(w2_v[0], U_FB, N_FF)
            sp.wait_ge(spatial_add_ready, GM)
            sp.dma_start(v_bias, gmlp_b_uv[0, GW:2 * GW].partition_broadcast(P)).then_inc(vb_landed, 16)
            with sp.Fori(0, N_GV // 4) as i:
                for j in range(8):
                    c = GW + (2 * i + j // 4) * RW
                    load(2 * U_GV + j, i, w_uv_v[:, 2 * (j % 4):2 * (j % 4) + 2, bass.ds(c, RW)])
            load_tables(2)
            load_tall(w_uv_v, U_GU, N_GU)
            load_rows(w_go_v, U_GO, N_GO)
            load_tall(w1_v[1], U_FC, N_FF)
            load_tables(3)
            load_rows(w2_v[1], U_FD, N_FF)
            for t in range(NT):
                for n in range(2):
                    sp.wait_ge(ln_done, 4 * (LNS - 1) + 2 * t + n + 1)
                    s = slice(n * HALF_D, (n + 1) * HALF_D)
                    sp.dma_start(out_v[:, t, s], resid[:, t, s]).then_inc(out_written[2 * t + n], 16)
            for s in out_written:
                sp.wait_ge(s, 16)

        @block.gpsimd
        def _(pool):
            step = Count(pool, pool_step)
            pool.dma_start(pos_i[:, :], positions.rearrange("a (t p) -> p (a t)", p=P),
                           allow_slow_non_contiguous=True) \
                .then_inc(rope_in_landed, 16)
            pool.dma_start(freq[:, :], inv_freq.partition_broadcast(P)).then_inc(freq_landed, 16)
            step.inc(nc.gpsimd.memset(ident[:, :], 0.0))
            step.inc(nc.gpsimd.memset(causal, 0.0))
            nc.gpsimd.memset(ones[:, :], 1.0).then_inc(ones_ready, 1)
            step.wait()
            nc.gpsimd.affine_select(out=ident[:, :], in_=ident[:, :], compare_op=ALU.not_equal,
                                    fill=1.0, base=0, pattern=[[-1, P]], channel_multiplier=1) \
                .then_inc(consts_ready, 1)
            lower = causal[:, P:3 * P]
            nc.gpsimd.affine_select(out=lower, in_=lower, compare_op=ALU.is_ge, fill=MASKED, base=0,
                                    pattern=[[0, 2], [-1, P]], channel_multiplier=1) \
                .then_inc(consts_ready, 1)

            for g in range(4):
                for t in range(NT):
                    pool.wait_ge(rope_products, 3 * (NT * g + t) + 3)
                    if g >= 2:
                        pool.wait_ge(qk_turned, NT * (g - 2) + t + 1)
                    nc.gpsimd.tensor_tensor(qk_n[g % 2][:, t, :], work[:, t, 0:RW],
                                            work[:, t, RW:2 * RW], ALU.add).then_inc(rope_added, 1)

            pool.wait_ge(gain_landed, 16)
            for t in range(NT):
                pool.wait_ge(gate_silu, t + 1)
                nc.gpsimd.tensor_tensor(gate[:, t, :], gate[:, t, :], gn_gain, ALU.mult) \
                    .then_inc(gate_ready, 1)

            def squares(tile_base):
                with pool.Fori(0, FM // 8) as i:
                    for j in range(8):
                        pool.wait_ge(act_out, tile_base + 8 * i + j + 1)
                        h = hidden[:, bass.ds(8 * i + j, 1), :]
                        nc.gpsimd.tensor_tensor(h, h, h, ALU.mult).then_inc(hidden_ready, 1)

            squares(0)
            pool.wait_ge(ws_landed, 16)
            nc.gpsimd.affine_select(out=ws_n, in_=ws_n, compare_op=ALU.is_ge, fill=0.0, base=0,
                                    pattern=[[0, GROUPS], [-1, P]], channel_multiplier=1) \
                .then_inc(ws_masked, 1)
            with pool.Fori(0, GM // 8) as i:
                for j in range(8):
                    pool.wait_ge(act_out, FM + 8 * i + j + 1)
                    pool.wait_ge(mixed_ready, 8 * i + j + 1)
                    nc.gpsimd.tensor_tensor(hidden[:, bass.ds(8 * i + j, 1), :],
                                            mixed[:, j % 2:j % 2 + 1, :], u_tile[:, j % 2:j % 2 + 1, :],
                                            ALU.mult).then_inc(hidden_ready, 1)
            squares(FM + GM)

        @block.scalar
        def _(act):
            def ln_scalar(ln, t):
                act.wait_ge(ln_var, NT * ln + t + 1)
                nc.scalar.activation(ln_rstd[:, t:t + 1], ln_rstd[:, t:t + 1], ACT.Sqrt) \
                    .then_inc(ln_std, 1)
                if ln < LNS - 1:
                    for n in range(2):
                        xt_piece(ln + 1, t, n)

            def xt_piece(event, t, n):
                act.wait_ge(xt_turned, 4 * event + 2 * t + n + 1)
                nc.scalar.activation(xt_high[:, 4 * n:4 * n + 4, t * P:(t + 1) * P],
                                     ps_m[:, 2 * t + n, :].rearrange("p (k c) -> p k c", k=4),
                                     ACT.Copy).then_inc(xt_high_ready, 1)

            def qk_out(g):
                for t in range(NT):
                    act.wait_ge(qk_turned, NT * g + t + 1)
                    nc.scalar.activation(qk_t[g][:, :, t * P:(t + 1) * P],
                                         ps_m[:, 2 * (g % 2) + t, :].rearrange("p (k c) -> p k c", k=4),
                                         ACT.Copy).then_inc(qk_t_ready, 1)

            def v_out(g):
                act.wait_ge(w_used, 4 * (g + 1))
                for t in range(NT):
                    nc.scalar.activation(v_n[g][:, t, :], ps_m[:, 2 * (g % 2) + t, :],
                                         ACT.Copy).then_inc(v_ready, 1)

            def exps(batch):
                act.wait_ge(moba_max, batch + 1)
                for h in range(4 * batch, 4 * batch + 4):
                    for t, s in ((1, slice(0, 2 * P)), (0, slice(2 * P, 3 * P))):
                        c = t * HEADS + h
                        nc.scalar.activation(p_moba[:, h, s], p_moba[:, h, s], ACT.Exp,
                                             bias=neg_mx[:, c:c + 1], scale=QK_SCALE,
                                             accum_out=p_sum[:, c:c + 1]).then_inc(moba_exp, 1)

            def p_out(h):
                act.wait_ge(p_turned, h + 1)
                nc.scalar.activation(p_moba[:, h, :], ps_y[:, h % 2, 0:3 * P], ACT.Copy) \
                    .then_inc(p_t_ready, 1)

            for t in range(NT):
                for n in range(2):
                    xt_piece(0, t, n)
            for j in range(LOOK):
                split_high(act, 0, j)
            act.wait_ge(angles_ready, 1)
            nc.scalar.activation(sin2[:, :, 0:ROPE_HALF], ang[:, :, :], ACT.Sin, scale=-1.0) \
                .then_inc(rope_tab_ready, 1)
            nc.scalar.activation(sin2[:, :, ROPE_HALF:HD], ang[:, :, :], ACT.Sin) \
                .then_inc(rope_tab_ready, 1)
            for s in (slice(0, ROPE_HALF), slice(ROPE_HALF, HD)):
                nc.scalar.activation(cos2[:, :, s], turns[:, :, :], ACT.Sin) \
                    .then_inc(rope_tab_ready, 1)

            for j in range(2 * N_PROJ):
                ahead(split_high, act, 0, j)
                if j in (6, 10, 14, 18):
                    qk_out((j - 6) // 4)
                if j == 13:
                    exps(0)
                if j == 16:
                    exps(1)
                if j == 20:
                    v_out(VB)
                if j == 24:
                    v_out(VA)
                if 23 <= j < 27:
                    for h in (2 * (j - 23), 2 * (j - 23) + 1):
                        p_out(h)
            for t in range(NT):
                act.wait_ge(c_turned, t + 1)
                nc.scalar.activation(ht_high[:, :, t * P:(t + 1) * P],
                                     ps_y[:, t, :].rearrange("p (k c) -> p k c", k=4), ACT.Copy) \
                    .then_inc(c_high_ready, 1)
            act.wait_ge(gn_var, 1)
            nc.scalar.activation(gn_rstd, gn_rstd, ACT.Sqrt).then_inc(gn_std, 1)
            act.wait_ge(w_used, 4 * (GA + 1))
            for t in range(NT):
                nc.scalar.activation(gate[:, t, :], ps_m[:, 2 * (GA % 2) + t, :], ACT.Silu) \
                    .then_inc(gate_silu, 1)
            for j in range(4):
                ahead(split_high, act, U_OUT, j)
            for t in range(NT):
                act.wait_ge(c_turned, NT + t + 1)
                nc.scalar.activation(xt_high[:, 0:4, t * P:(t + 1) * P],
                                     ps_m[:, 2 + t, :].rearrange("p (k c) -> p k c", k=4), ACT.Copy) \
                    .then_inc(c_high_ready, 1)

            def tail(ln, unit_base):
                ahead(split_high, act, unit_base, 0)
                for t in range(NT):
                    ln_scalar(ln, t)
                for j in range(1, 4):
                    ahead(split_high, act, unit_base, j)

            tail(0, U_OUT + 2)

            def tall_stage(unit_base, n, tile_base, finish):
                with act.Fori(0, n // 4) as i:
                    for j in range(8):
                        ahead(split_high, act, unit_base, j, i)
                        act.wait_ge(w_used, 2 * unit_base + 8 * i + j + 1)
                        finish(i, j, ps_m[:, j % 4, 0:SEQ]).then_inc(act_out, 1)

            def relu_tile(i, j, bank):
                return nc.scalar.activation(hidden[:, bass.ds(8 * i + j, 1), :].rearrange("p a b -> p (a b)"),
                                            bank, ACT.Relu)

            def hidden_high(n, ready, half, i=0):
                act.wait_ge(hidden_ready, ready + n + 1 + 8 * i)
                act.wait_ge(w_used, half + n - 4 + 1 + 8 * i)
                src = hidden[:, n, :] if isinstance(i, int) and i == 0 else \
                    hidden[:, bass.ds(8 * i + n, 1), :].rearrange("p a b -> p (a b)")
                nc.scalar.activation(ht_high[:, n % 4, :], src, ACT.Copy).then_inc(ht_high_ready, 1)

            def rows_stage(ln, unit_base, tiles, ready, between=None):
                for n in range(2):
                    hidden_high(n, ready, 2 * unit_base)
                if between is not None:
                    between()
                loops = (tiles - 4) // 8
                if loops > 1:
                    with act.Fori(0, loops) as i:
                        for j in range(8):
                            ahead(split_high, act, unit_base, j, i)
                            hidden_high(j + 2, ready, 2 * unit_base, i)
                for n in range(8 * loops if loops > 1 else 0, tiles - 4):
                    ahead(split_high, act, unit_base, n)
                    hidden_high(n + 2, ready, 2 * unit_base)
                for n in range(tiles - 2, tiles):
                    hidden_high(n, ready, 2 * unit_base)
                tail(ln, unit_base + tiles // 2 - 2)

            def small_tables():
                act.wait_ge(ws_turned, 3)
                nc.scalar.activation(cols48[:, :], ps_m[:, 2, 0:3 * GM], ACT.Copy).then_inc(ws_t_ready, 1)
                for b in range(2):
                    nc.scalar.activation(ws_t[:, 4 * b:4 * b + 4, :],
                                         ps_m[:, b, :].rearrange("p (g c) -> p g c", g=4),
                                         ACT.Copy).then_inc(ws_t_ready, 1)

            tall_stage(U_FA, N_FF, 0, relu_tile)
            rows_stage(1, U_FB, FM, 0, small_tables)

            with act.Fori(0, N_GV // 4) as i:
                for j in range(8):
                    ahead(split_high, act, U_GV, j, i)
                    if j % 4 == 3:
                        for t in range(NT):
                            act.wait_ge(v_biased, 4 * i + 2 * (j // 4) + t + 1)
                            v = v_gate[:, t, bass.ds((2 * i + j // 4) * RW, RW)]
                            nc.scalar.activation(v, v, ACT.Gelu_apprx_tanh).then_inc(v_gelu, 1)
            act.wait_ge(v_var, 1)
            nc.scalar.activation(v_rstd, v_rstd, ACT.Sqrt).then_inc(v_std, 1)
            with act.Fori(0, N_GU // 4) as i:
                for j in range(8):
                    ahead(split_high, act, U_GU, j, i)
                    act.wait_ge(w_used, 2 * U_GU + 8 * i + j + 1)
                    act.wait_ge(hidden_ready, FM - 1 + 8 * i + j)
                    nc.scalar.activation(u_tile[:, j % 2, :], ps_m[:, j % 4, 0:SEQ], ACT.Gelu_apprx_tanh,
                                         bias=cols48[:, bass.ds(8 * i + j, 1)]).then_inc(act_out, 1)
            rows_stage(2, U_GO, GM, FM)
            tall_stage(U_FC, N_FF, FM + GM, relu_tile)
            rows_stage(3, U_FD, FM, FM + GM)

        @block.vector
        def _(dve):
            step = Count(dve, dve_step)
            dve.wait_ge(rope_in_landed, 16)
            step.inc(nc.vector.tensor_copy(pos_f, pos_i[:, :]))
            dve.wait_ge(freq_landed, 16)
            step.wait()
            for t in range(NT):
                step.inc(nc.vector.tensor_scalar(ang[:, t, :], freq[:, :], pos_f[:, t:t + 1], None, ALU.mult))
            step.wait()
            magic = 1.5 * 2.0 ** 23
            for level, parts in ((24, 6), (12, 5), (0, 4)):
                period = 2.0 * np.pi * 2.0 ** level
                step.inc(nc.vector.tensor_scalar(turns[:, :, :], ang[:, :, :], float(1.0 / period), magic,
                                                 ALU.mult, ALU.add))
                step.wait()
                step.inc(nc.vector.tensor_scalar(turns[:, :, :], turns[:, :, :], magic, None, ALU.subtract))
                step.wait()
                for part in split_bits(period, 11, parts):
                    step.inc(nc.vector.scalar_tensor_tensor(out=ang[:, :, :], in0=turns[:, :, :], scalar=-part,
                                                            in1=ang[:, :, :], op0=ALU.mult, op1=ALU.add))
                    step.wait()
            pi_below = 3.1415925
            step.inc(nc.vector.tensor_scalar(ang[:, :, :], ang[:, :, :], pi_below, -pi_below, ALU.min, ALU.max))
            step.wait()
            step.inc(nc.vector.scalar_tensor_tensor(out=turns[:, :, :], in0=ang[:, :, :], scalar=-1.0,
                                                    in1=ang[:, :, :], op0=ALU.mult, op1=ALU.min))
            step.wait()
            nc.vector.tensor_scalar(turns[:, :, :], turns[:, :, :], float(np.pi / 2), None, ALU.add) \
                .then_inc(angles_ready, 1)

            def xt_piece(event, t, n):
                dve.wait_ge(xt_high_ready, 4 * event + 2 * t + n + 1)
                s = (slice(None), slice(4 * n, 4 * n + 4), slice(t * P, (t + 1) * P))
                nc.vector.tensor_tensor(xt_low[s], ps_m[:, 2 * t + n, :].rearrange("p (k c) -> p k c", k=4),
                                        xt_high[s], ALU.subtract).then_inc(xt_low_ready, 1)

            def rstd_of(var, out_cols):
                step.inc(nc.vector.tensor_scalar(out_cols, var, EPS, None, ALU.add))
                step.wait()
                return nc.vector.reciprocal(out_cols, out_cols)

            def layer_norm(ln, t, end):
                added = []
                for n in range(2):
                    s = slice(n * HALF_D, (n + 1) * HALF_D)
                    if (t, n) == (1, 1):
                        dve.wait_ge(w_used, end)
                    else:
                        dve.wait_ge(y_done, 2 * ln + 1 + t)
                    added.append(step.inc(nc.vector.scalar_tensor_tensor(
                        out=work[:, t, s], in0=resid[:, t, s], scalar=ALPHA, in1=ps_y[:, 2 * t + n, :],
                        op0=ALU.mult, op1=ALU.add)))
                    step.wait(added[n])
                    c = 6 * (2 * t + n)
                    step.inc(nc.vector.bn_stats(ln_stats[:, c:c + 6], work[:, t, s]))
                step.wait()
                mv = ln_mv[:, 2 * t:2 * t + 2]
                step.inc(nc.vector.bn_aggr(mv, ln_stats[:, 12 * t:12 * t + 12]))
                step.wait()
                rstd_of(mv[:, 1:2], ln_rstd[:, t:t + 1]).then_inc(ln_var, 1)
                if t == 0:
                    dve.wait_ge(tab_landed, 16 * (ln + 1))
                    dve.wait_ge(tab2_landed, 16 * (ln + 1))
                for n in range(2):
                    s = slice(n * HALF_D, (n + 1) * HALF_D)
                    step.inc(nc.vector.scalar_tensor_tensor(out=work[:, t, s], in0=work[:, t, s],
                                                            scalar=mv[:, 0:1], in1=ln_tab[:, 0, s],
                                                            op0=ALU.subtract, op1=ALU.mult))
                dve.wait_ge(ln_std, NT * ln + t + 1)
                step.wait()
                for n in range(2):
                    s = slice(n * HALF_D, (n + 1) * HALF_D)
                    nc.vector.scalar_tensor_tensor(out=resid[:, t, s], in0=work[:, t, s],
                                                   scalar=ln_rstd[:, t:t + 1], in1=ln_tab[:, 1, s],
                                                   op0=ALU.mult, op1=ALU.add).then_inc(ln_done, 1)
                if ln < LNS - 1:
                    for n in range(2):
                        xt_piece(ln + 1, t, n)

            for t in range(NT):
                for n in range(2):
                    xt_piece(0, t, n)
            for j in range(LOOK):
                split_low(dve, 0, j)

            def rope(g):
                dve.wait_ge(w_used, 4 * (g + 1))
                if g == 0:
                    dve.wait_ge(rope_tab_ready, 4)
                for t in range(NT):
                    if g > 0:
                        dve.wait_ge(rope_added, NT * (g - 1) + t + 1)
                    src = ps_m[:, 2 * (g % 2) + t, :].rearrange("p (h d) -> p h d", h=HEADS)
                    a = work[:, t, 0:RW].rearrange("p (h d) -> p h d", h=HEADS)
                    b = work[:, t, RW:2 * RW].rearrange("p (h d) -> p h d", h=HEADS)
                    wide_cos = cos2[:, t:t + 1, :].to_broadcast([P, HEADS, HD])
                    wide_sin = sin2[:, t:t + 1, :].to_broadcast([P, HEADS, HD])
                    nc.vector.tensor_tensor(a, src, wide_cos, ALU.mult).then_inc(rope_products, 1)
                    for to, of in ((slice(0, ROPE_HALF), slice(ROPE_HALF, HD)),
                                   (slice(ROPE_HALF, HD), slice(0, ROPE_HALF))):
                        nc.vector.tensor_tensor(b[:, :, to], src[:, :, of], wide_sin[:, :, to],
                                                ALU.mult).then_inc(rope_products, 1)

            def moba_mask(batch):
                if batch == 0:
                    dve.wait_ge(consts_ready, 2)
                for h in range(4 * batch, 4 * batch + 4):
                    dve.wait_ge(moba_scores, h + 1)
                    nc.vector.tensor_tensor(p_moba[:, h, :], ps_y[:, h % 4, 0:3 * P], causal,
                                            ALU.add).then_inc(moba_masked, 1)
                hs = slice(4 * batch, 4 * batch + 4)
                dve.wait_ge(moba_masked, 4 * batch + 4)
                for t, s in ((1, slice(0, 2 * P)), (0, slice(2 * P, 3 * P))):
                    step.inc(nc.vector.tensor_reduce(mx[:, t * HEADS:(t + 1) * HEADS][:, hs], p_moba[:, hs, s],
                                                     AX_X, ALU.max))
                step.wait()
                two = lambda c: c.rearrange("p (t h) -> p t h", t=2)[:, :, hs]
                nc.vector.tensor_scalar(two(neg_mx), two(mx), -QK_SCALE, None, ALU.mult).then_inc(moba_max, 1)

            def ret_decay(batch):
                if batch == 0:
                    dve.wait_ge(decay_landed, 16)
                for h in range(4 * batch, 4 * batch + 4):
                    dve.wait_ge(ret_scores, h + 1)
                    nc.vector.tensor_tensor(p_ret[:, h, 0:2 * P], ps_y[:, h % 4, 0:2 * P],
                                            decay_t[:, h, :], ALU.mult)
                    nc.vector.tensor_tensor(p_ret[:, h, 2 * P:3 * P], ps_y[:, h % 4, 2 * P:3 * P],
                                            decay_t[:, h, 0:P], ALU.mult).then_inc(ret_decayed, 1)

            def per_head(c):
                return c.unsqueeze(2).to_broadcast([P, HEADS, HD])

            for j in range(2 * N_PROJ):
                ahead(split_low, dve, 0, j)
                if j in (4, 8, 12, 16):
                    rope(j // 4 - 1)
                if j == 12:
                    moba_mask(0)
                if j == 15:
                    moba_mask(1)
                if j == 20:
                    ret_decay(0)
                if j == 22:
                    ret_decay(1)
                if j == 27:
                    dve.wait_ge(moba_exp, 2 * HEADS)
                    step.inc(nc.vector.reciprocal(p_inv, p_sum))
                    step.wait()
                    dve.wait_ge(moba_out, 1)
                    for t in range(NT):
                        nc.vector.tensor_tensor(y_moba[:, t, :].rearrange("p (h d) -> p h d", h=HEADS),
                                                ps_y[:, 2 + t, :].rearrange("p (h d) -> p h d", h=HEADS),
                                                per_head(p_inv[:, t * HEADS:(t + 1) * HEADS]),
                                                ALU.mult).then_inc(y_moba_ready, 1)
            for t in range(NT):
                dve.wait_ge(c_high_ready, t + 1)
                nc.vector.tensor_tensor(ht_low[:, :, t * P:(t + 1) * P],
                                        ps_y[:, t, :].rearrange("p (k c) -> p k c", k=4),
                                        ht_high[:, :, t * P:(t + 1) * P], ALU.subtract) \
                    .then_inc(c_low_ready, 1)
            dve.wait_ge(ret_out, 1)
            for t in range(NT):
                for h in range(HEADS):
                    c = 6 * (t * HEADS + h)
                    step.inc(nc.vector.bn_stats(gn_stats[:, c:c + 6], ps_m[:, 2 + t, h * HD:(h + 1) * HD]))
            step.wait()
            for c in range(2 * HEADS):
                step.inc(nc.vector.bn_aggr(gn_mv[:, 2 * c:2 * c + 2], gn_stats[:, 6 * c:6 * c + 6]))
            step.wait()
            gn_pairs = gn_mv.rearrange("p (c two) -> p c two", two=2)
            rstd_of(gn_pairs[:, :, 1], gn_rstd).then_inc(gn_var, 1)
            for t in range(NT):
                y = y_ret[:, t, :].rearrange("p (h d) -> p h d", h=HEADS)
                s = slice(t * HEADS, (t + 1) * HEADS)
                step.inc(nc.vector.tensor_tensor(y, ps_m[:, 2 + t, :].rearrange("p (h d) -> p h d", h=HEADS),
                                                 per_head(gn_pairs[:, s, 0]), ALU.subtract))
            dve.wait_ge(gn_std, 1)
            step.wait()
            for t in range(NT):
                y = y_ret[:, t, :].rearrange("p (h d) -> p h d", h=HEADS)
                step.inc(nc.vector.tensor_tensor(y, y, per_head(gn_rstd[:, t * HEADS:(t + 1) * HEADS]), ALU.mult))
            step.wait()
            for t in range(NT):
                dve.wait_ge(gate_ready, t + 1)
                nc.vector.tensor_tensor(y_ret[:, t, :], y_ret[:, t, :], gate[:, t, :],
                                        ALU.mult).then_inc(y_ret_ready, 1)
            for j in range(4):
                ahead(split_low, dve, U_OUT, j)
            for t in range(NT):
                dve.wait_ge(c_high_ready, NT + t + 1)
                nc.vector.tensor_tensor(xt_low[:, 0:4, t * P:(t + 1) * P],
                                        ps_m[:, 2 + t, :].rearrange("p (k c) -> p k c", k=4),
                                        xt_high[:, 0:4, t * P:(t + 1) * P], ALU.subtract) \
                    .then_inc(c_low_ready, 1)

            def tail(ln, unit_base):
                ahead(split_low, dve, unit_base, 0)
                for t in range(NT):
                    layer_norm(ln, t, 2 * unit_base + 4)
                for j in range(1, 4):
                    ahead(split_low, dve, unit_base, j)

            tail(0, U_OUT + 2)

            def tall_stage(unit_base, n):
                with dve.Fori(0, n // 4) as i:
                    for j in range(8):
                        ahead(split_low, dve, unit_base, j, i)

            def hidden_low(n, seen, i=0):
                dve.wait_ge(ht_high_ready, seen + n + 1 + 8 * i)
                src = hidden[:, n, :] if isinstance(i, int) and i == 0 else \
                    hidden[:, bass.ds(8 * i + n, 1), :].rearrange("p a b -> p (a b)")
                nc.vector.tensor_tensor(ht_low[:, n % 4, :], src, ht_high[:, n % 4, :], ALU.subtract) \
                    .then_inc(ht_low_ready, 1)

            def rows_stage(ln, unit_base, tiles, seen, between=None):
                for n in range(2):
                    hidden_low(n, seen)
                loops = (tiles - 4) // 8
                if loops > 1:
                    with dve.Fori(0, loops) as i:
                        for j in range(8):
                            ahead(split_low, dve, unit_base, j, i)
                            hidden_low(j + 2, seen, i)
                if between is not None:
                    between()
                for n in range(8 * loops if loops > 1 else 0, tiles - 4):
                    ahead(split_low, dve, unit_base, n)
                    hidden_low(n + 2, seen)
                for n in range(tiles - 2, tiles):
                    hidden_low(n, seen)
                tail(ln, unit_base + tiles // 2 - 2)

            def spatial_table():
                dve.wait_ge(row_sums, 2)
                dve.wait_ge(bs_landed, 16)
                dve.wait_ge(ws_t_ready, 3)
                for m in range(GM):
                    g = m // 2
                    bank = 3 if g < 4 else 0
                    nc.vector.scalar_tensor_tensor(out=spatial_add[:, m, :],
                                                   in0=ps_m[:, bank, (g % 4) * P:(g % 4 + 1) * P],
                                                   scalar=cols48[:, 2 * GM + m:2 * GM + m + 1],
                                                   in1=b_s_all[:, g, :], op0=ALU.mult, op1=ALU.add) \
                        .then_inc(spatial_add_ready, 1)

            tall_stage(U_FA, N_FF)
            rows_stage(1, U_FB, FM, 0, spatial_table)

            dve.wait_ge(vb_landed, 16)
            with dve.Fori(0, N_GV // 4) as i:
                for j in range(8):
                    ahead(split_low, dve, U_GV, j, i)
                    if j % 4 == 3:
                        g = j // 4
                        dve.wait_ge(w_used, 2 * U_GV + 8 * i + j + 1)
                        for t in range(NT):
                            nc.vector.tensor_tensor(v_gate[:, t, bass.ds((2 * i + g) * RW, RW)],
                                                    ps_m[:, 2 * g + t, :], v_bias[:, bass.ds((2 * i + g) * RW, RW)],
                                                    ALU.add).then_inc(v_biased, 1)
                        for t in range(NT):
                            dve.wait_ge(v_gelu, 4 * i + 2 * g + t + 1)
                            nc.vector.bn_stats(v_stats[:, bass.ds(24 * t + 6 * (2 * i + g), 6)],
                                               v_gate[:, t, bass.ds((2 * i + g) * RW, RW)]).then_inc(v_stat, 1)
            dve.wait_ge(v_stat, 4 * NT)
            for t in range(NT):
                step.inc(nc.vector.bn_aggr(v_mv[:, 2 * t:2 * t + 2], v_stats[:, 24 * t:24 * t + 24]))
            step.wait()
            rstd_of(v_mv.rearrange("p (t two) -> p t two", two=2)[:, :, 1], v_rstd).then_inc(v_var, 1)
            dve.wait_ge(v_std, 1)

            def normalise(m, i):
                for t in range(NT):
                    nc.vector.tensor_scalar(vn_tile[:, m % 2, t, :], v_gate[:, t, bass.ds((8 * i + m) * P, P)],
                                            v_mv[:, 2 * t:2 * t + 1], v_rstd[:, t:t + 1],
                                            ALU.subtract, ALU.mult).then_inc(vn_ready, 1)

            def mix(m, i):
                dve.wait_ge(spatial_done, m + 1 + 8 * i)
                dve.wait_ge(hidden_ready, FM - 1 + m + 8 * i)
                tile = bass.ds(8 * i + m, 1)
                nc.vector.scalar_tensor_tensor(
                    out=mixed[:, m % 2, :].rearrange("p (t c) -> p t c", t=NT),
                    in0=ps_y[:, m % 4, 0:SEQ].rearrange("p (t c) -> p t c", t=NT),
                    scalar=cols48[:, bass.ds(8 * i + (GM + m), 1)],
                    in1=spatial_add[:, tile, :].to_broadcast([P, NT, P]),
                    op0=ALU.mult, op1=ALU.add).then_inc(mixed_ready, 1)

            dve.wait_ge(spatial_add_ready, GM)
            with dve.Fori(0, N_GU // 4) as i:
                for j in range(8):
                    ahead(split_low, dve, U_GU, j, i)
                    normalise(j, i)
                    mix(j, i)
            rows_stage(2, U_GO, GM, FM)
            tall_stage(U_FC, N_FF)
            rows_stage(3, U_FD, FM, FM + GM)

        @block.tensor
        def _(pe):
            def turn(bank, src, n=4):
                for c in range(n):
                    last = nc.tensor.transpose(bank[:, c * P:(c + 1) * P], src[:, c * P:(c + 1) * P], ident[:, :])
                return last

            def turn_resid(event):
                for t in range(NT):
                    for n in range(2):
                        if event == 0:
                            pe.wait_ge(x_landed[t], 16)
                        else:
                            pe.wait_ge(ln_done, 4 * (event - 1) + 2 * t + n + 1)
                        turn(ps_m[:, 2 * t + n, :], resid[:, t, n * HALF_D:(n + 1) * HALF_D]) \
                            .then_inc(xt_turned, 1)

            def wide_half(slot, quarter, banks):
                hi, lo = wide(w_high, slot), wide(w_low, slot)
                for k in (2 * quarter, 2 * quarter + 1):
                    k4 = k % 4
                    for t in range(NT):
                        s = slice(t * P, (t + 1) * P)
                        out_b = banks[t]
                        nc.tensor.matmul(out_b, xt_high[:, k, s], hi[:, k4, :], start=(k == 0), stop=False)
                        nc.tensor.matmul(out_b, xt_high[:, k, s], lo[:, k4, :], start=False, stop=False)
                        mm = nc.tensor.matmul(out_b, xt_low[:, k, s], hi[:, k4, :], start=False,
                                              stop=(k == KD - 1))
                return mm

            pe.wait_ge(consts_ready, 1)
            turn_resid(0)

            def turn_qk(g):
                for t in range(NT):
                    pe.wait_ge(rope_added, NT * g + t + 1)
                    turn(ps_m[:, 2 * (g % 2) + t, :], qk_n[g % 2][:, t, :]).then_inc(qk_turned, 1)

            def scores_moba(pair):
                for h in (2 * pair, 2 * pair + 1):
                    rows = slice((h % 2) * HD, (h % 2 + 1) * HD)
                    if h >= 4:
                        pe.wait_ge(moba_masked, h - 3)
                    q, k = qk_t[QB][rows, pair, :], qk_t[KB][rows, pair, :]
                    bank = ps_y[:, h % 4, :]
                    nc.tensor.matmul(bank[:, 0:2 * P], q[:, P:2 * P], k[:, 0:2 * P], start=True, stop=True)
                    nc.tensor.matmul(bank[:, 2 * P:3 * P], q[:, 0:P], k[:, 0:P], start=True, stop=True) \
                        .then_inc(moba_scores, 1)

            def scores_ret(pair):
                for h in (2 * pair, 2 * pair + 1):
                    rows = slice((h % 2) * HD, (h % 2 + 1) * HD)
                    if h < 4:
                        pe.wait_ge(moba_masked, HEADS)
                    else:
                        pe.wait_ge(ret_decayed, h - 3)
                    q, k = qk_t[QA][rows, pair, :], qk_t[KA][rows, pair, :]
                    bank = ps_y[:, h % 4, :]
                    nc.tensor.matmul(bank[:, 0:2 * P], k[:, 0:P], q[:, 0:2 * P], start=True, stop=True)
                    nc.tensor.matmul(bank[:, 2 * P:3 * P], k[:, P:2 * P], q[:, P:2 * P], start=True, stop=True) \
                        .then_inc(ret_scores, 1)

            def turn_p(h):
                pe.wait_ge(moba_exp, 2 * h + 2)
                if h < 2:
                    pe.wait_ge(ret_decayed, HEADS - 2)
                else:
                    pe.wait_ge(p_t_ready, h - 1)
                turn(ps_y[:, h % 2, :], p_moba[:, h, :], 3).then_inc(p_turned, 1)

            def values_moba():
                pe.wait_ge(v_ready, NT)
                pe.wait_ge(ret_decayed, HEADS)
                for h in range(HEADS):
                    pe.wait_ge(p_t_ready, h + 1)
                    c = slice(h * HD, (h + 1) * HD)
                    w = p_moba[:, h, :]
                    nc.tensor.matmul(ps_y[:, 3, c], w[:, 0:P], v_n[VB][:, 0, c], start=True, stop=False)
                    nc.tensor.matmul(ps_y[:, 3, c], w[:, P:2 * P], v_n[VB][:, 1, c], start=False, stop=True)
                    mm = nc.tensor.matmul(ps_y[:, 2, c], w[:, 2 * P:3 * P], v_n[VB][:, 0, c],
                                          start=True, stop=True)
                mm.then_inc(moba_out, 1)

            def values_ret():
                pe.wait_ge(v_ready, 2 * NT)
                for h in range(HEADS):
                    c = slice(h * HD, (h + 1) * HD)
                    w = p_ret[:, h, :]
                    nc.tensor.matmul(ps_m[:, 2, c], w[:, 0:P], v_n[VA][:, 0, c], start=True, stop=True)
                    nc.tensor.matmul(ps_m[:, 3, c], w[:, P:2 * P], v_n[VA][:, 0, c], start=True, stop=False)
                    mm = nc.tensor.matmul(ps_m[:, 3, c], w[:, 2 * P:3 * P], v_n[VA][:, 1, c],
                                          start=False, stop=True)
                mm.then_inc(ret_out, 1)

            pe.wait_ge(xt_low_ready, 4)
            for j in range(2 * N_PROJ):
                g, q = j // 4, j % 4
                if q == 0 and g >= 2:
                    if g - 2 < 4:
                        pe.wait_ge(qk_t_ready, NT * (g - 1))
                    else:
                        pe.wait_ge(v_ready, NT)
                pe.wait_ge(w_low_ready, j + 1)
                wide_half((j // 2) % SLOTS, q, [ps_m[:, 2 * (g % 2) + t, :] for t in range(NT)]) \
                    .then_inc(w_used, 1)
                if j in (5, 9, 13, 17):
                    turn_qk((j - 5) // 4)
                if j == 11:
                    pe.wait_ge(qk_t_ready, 2 * NT)
                    scores_moba(0)
                    scores_moba(1)
                if j == 14:
                    scores_moba(2)
                    scores_moba(3)
                if j == 19:
                    pe.wait_ge(qk_t_ready, 4 * NT)
                    scores_ret(0)
                    scores_ret(1)
                if j == 21:
                    scores_ret(2)
                    scores_ret(3)
                if 22 <= j < 26:
                    turn_p(2 * (j - 22))
                    turn_p(2 * (j - 22) + 1)
                if j == 26:
                    values_moba()
                    values_ret()

            for t in range(NT):
                pe.wait_ge(y_moba_ready, t + 1)
                turn(ps_y[:, t, :], y_moba[:, t, :]).then_inc(c_turned, 1)

            def rows_products(stationary, t, n, slot, half, start, stop):
                (hi, lo) = stationary
                s = slice(t * P, (t + 1) * P)
                c = slice(n * HALF_D, (n + 1) * HALF_D)
                bank = ps_y[:, 2 * t + n, :]
                wh, wl = flat(w_high, slot, half)[:, c], flat(w_low, slot, half)[:, c]
                nc.tensor.matmul(bank, hi[:, s], wh, start=start, stop=False)
                nc.tensor.matmul(bank, hi[:, s], wl, start=False, stop=False)
                return nc.tensor.matmul(bank, lo[:, s], wh, start=False, stop=stop)

            def rows_half(unit_base, j, stationary, start):
                for t in range(NT):
                    for n in range(2):
                        mm = rows_products(stationary, t, n, (unit_base + j // 2) % SLOTS, j % 2, start, False)
                mm.then_inc(w_used, 1)

            def rows_tail(unit_base, stationary, ready):
                for t, n_set in ((0, (0, 1)), (1, (0,)), (1, (1,))):
                    for j in range(4):
                        if t == 0:
                            pe.wait_ge(w_low_ready, 2 * unit_base + j + 1)
                            ready(j)
                        for n in n_set:
                            mm = rows_products(stationary(j), t, n, (unit_base + j // 2) % SLOTS, j % 2,
                                               False, j == 3)
                        if (t, n) == (1, 1):
                            mm.then_inc(w_used, 1)
                    if (t, n) != (1, 1):
                        mm.then_inc(y_done, 1)

            pe.wait_ge(c_low_ready, NT)
            for j in range(4):
                pe.wait_ge(w_low_ready, 2 * U_OUT + j + 1)
                rows_half(U_OUT, j, (ht_high[:, j, :], ht_low[:, j, :]), j == 0)
            for t in range(NT):
                pe.wait_ge(y_ret_ready, t + 1)
                turn(ps_m[:, 2 + t, :], y_ret[:, t, :]).then_inc(c_turned, 1)
            pe.wait_ge(c_low_ready, 2 * NT)
            rows_tail(U_OUT + 2, lambda j: (xt_high[:, j, :], xt_low[:, j, :]), lambda j: None)
            turn_resid(1)

            def tall_products(slot, half, bank):
                hi, lo = tall(w_high, slot, half), tall(w_low, slot, half)
                for k in range(KD):
                    nc.tensor.matmul(bank, hi[:, k, :], xt_high[:, k, :], start=(k == 0), stop=False)
                    nc.tensor.matmul(bank, hi[:, k, :], xt_low[:, k, :], start=False, stop=False)
                    mm = nc.tensor.matmul(bank, lo[:, k, :], xt_high[:, k, :], start=False, stop=(k == KD - 1))
                return mm

            def tall_stage(unit_base, n, tile_base):
                def tile(i, j):
                    pe.wait_ge(w_low_ready, 2 * unit_base + 8 * i + j + 1)
                    if not (isinstance(i, int) and tile_base + 8 * i + j < 4):
                        pe.wait_ge(act_out, tile_base + 8 * i + j - 3)
                    tall_products((unit_base + j // 2) % SLOTS, j % 2, ps_m[:, j % 4, 0:SEQ]) \
                        .then_inc(w_used, 1)

                for j in range(8):
                    tile(0, j)
                with pe.Fori(1, n // 4) as i:
                    for j in range(8):
                        tile(i, j)

            def rows_stage(unit_base, tiles, seen, between=None):
                def ready(j, i=0):
                    pe.wait_ge(ht_low_ready, seen + j + 1 + 8 * i)

                for j in range(4):
                    pe.wait_ge(w_low_ready, 2 * unit_base + j + 1)
                    ready(j)
                    rows_half(unit_base, j, (ht_high[:, j, :], ht_low[:, j, :]), j == 0)
                if between is not None:
                    between()
                loops = (tiles - 8) // 8
                if loops > 1:
                    with pe.Fori(0, loops) as i:
                        for j in range(4, 12):
                            pe.wait_ge(w_low_ready, 2 * unit_base + 8 * i + j + 1)
                            ready(j, i)
                            rows_half(unit_base, j, (ht_high[:, j % 4, :], ht_low[:, j % 4, :]), False)
                for j in range(4 + (8 * loops if loops > 1 else 0), tiles - 4):
                    pe.wait_ge(w_low_ready, 2 * unit_base + j + 1)
                    ready(j)
                    rows_half(unit_base, j, (ht_high[:, j % 4, :], ht_low[:, j % 4, :]), False)
                rows_tail(unit_base + tiles // 2 - 2, lambda j: (ht_high[:, j, :], ht_low[:, j, :]),
                          lambda j: ready(tiles - 4 + j))

            def row_sum_products():
                pe.wait_ge(ones_ready, 1)
                pe.wait_ge(ws_t_ready, 3)
                for b, bank in ((0, 3), (1, 0)):
                    nc.tensor.matmul(ps_m[:, bank, :], ones[:, :],
                                     ws_t[:, 4 * b:4 * b + 4, :].rearrange("p g c -> p (g c)"),
                                     start=True, stop=True).then_inc(row_sums, 1)

            pe.wait_ge(xt_low_ready, 8)
            tall_stage(U_FA, N_FF, 0)
            pe.wait_ge(act_out, FM)
            pe.wait_ge(ws_masked, 1)
            for b in range(2):
                turn(ps_m[:, b, :], ws_n[:, 4 * b:4 * b + 4, :].rearrange("p g c -> p (g c)")) \
                    .then_inc(ws_turned, 1)
            for s in rows_landed:
                pe.wait_ge(s, 16)
            nc.tensor.transpose(ps_m[:, 2, 0:3 * GM], rows48[:, :], ident[0:3 * GM, 0:3 * GM]) \
                .then_inc(ws_turned, 1)
            rows_stage(U_FB, FM, 0, row_sum_products)
            pe.wait_ge(spatial_add_ready, GM)
            turn_resid(2)

            pe.wait_ge(xt_low_ready, 12)
            for j in range(2 * N_GV):
                g, q = j // 4, j % 4
                if q == 0 and g >= 2:
                    pe.wait_ge(v_biased, NT * (g - 1))
                pe.wait_ge(w_low_ready, 2 * U_GV + j + 1)
                wide_half((U_GV + j // 2) % SLOTS, q, [ps_m[:, 2 * (g % 2) + t, :] for t in range(NT)]) \
                    .then_inc(w_used, 1)
            pe.wait_ge(v_biased, 4 * NT)
            with pe.Fori(0, N_GU // 4) as i:
                for j in range(8):
                    pe.wait_ge(w_low_ready, 2 * U_GU + 8 * i + j + 1)
                    pe.wait_ge(act_out, FM + 8 * i + j - 3)
                    tall_products((U_GU + j // 2) % SLOTS, j % 2, ps_m[:, j % 4, 0:SEQ]) \
                        .then_inc(w_used, 1)
                    pe.wait_ge(vn_ready, 2 * (8 * i + j) + 2)
                    pe.wait_ge(hidden_ready, FM + 8 * i + j - 3)
                    for t in range(NT):
                        mm = nc.tensor.matmul(ps_y[:, j % 4, t * P:(t + 1) * P], vn_tile[:, j % 2, t, :],
                                              ws_t[:, bass.ds(4 * i + j // 2, 1), :].rearrange("p a b -> p (a b)"),
                                              start=True, stop=True)
                    mm.then_inc(spatial_done, 1)
            pe.wait_ge(mixed_ready, GM)
            rows_stage(U_GO, GM, FM)
            turn_resid(3)

            pe.wait_ge(xt_low_ready, 16)
            tall_stage(U_FC, N_FF, FM + GM)
            rows_stage(U_FD, FM, FM + GM)


_INS = ["x", "positions", "ln_gain", "ln_bias", "mix_w_in", "ret_gn_gain", "mix_w_out", "gmlp_w_uv",
        "gmlp_b_uv", "gmlp_ln_gain", "gmlp_ln_bias", "gmlp_w_s", "gmlp_b_s", "gmlp_w_out", "ffn_w_in",
        "ffn_w_out"]


def shape_constants():
    freq = (10000.0 ** (-np.arange(0, HD, 2) / HD)).astype(np.float32)
    gamma = 1.0 - 2.0 ** (-5.0 - np.arange(HEADS))
    diff = np.arange(SEQ)[None, None, :] - np.arange(P)[:, None, None]
    decay = np.where(diff >= 0, gamma[None, :, None] ** np.maximum(diff, 0), 0.0) * QK_SCALE
    return freq, decay.astype(np.float32).reshape(P, HEADS * SEQ)


def kernel(**inputs):
    import concourse.bacc as bacc
    from concourse.bass_utils import run_bass_kernel_spmd

    nc = bacc.Bacc("TRN2", target_bir_lowering=False, num_devices=1)
    arrays = {name: np.ascontiguousarray(inputs[name]) for name in _INS}
    arrays["inv_freq"], arrays["decay"] = shape_constants()
    args = [nc.dram_tensor(f"in_{name}", a.shape, mybir.dt.from_np(a.dtype), kind="ExternalInput").ap()
            for name, a in arrays.items()]
    args.append(nc.dram_tensor("out_0", (1, SEQ, D), F32, kind="ExternalOutput").ap())
    build(nc, *args)
    r = run_bass_kernel_spmd(nc, [{f"in_{name}": a for name, a in arrays.items()}], core_ids=[0])
    return r.results[0]["out_0"]
```

```python
from contextlib import ExitStack

import numpy as np

import concourse.bass as bass
from concourse import mybir

F32 = mybir.dt.float32
F32R = mybir.dt.float32r
I32 = mybir.dt.int32
ALU = mybir.AluOpType
ACT = mybir.ActivationFunctionType
AX_X = mybir.AxisListType.X

P = 128
SEQ = 256
NT = SEQ // P
D = 1024
KD = D // P
HALF_D = D // 2
HEADS = 8
HD = 64
HEAD_PAIRS = HEADS // 2
ROPE_HALF = HD // 2
RW = HEADS * HD
GROUPS = 8
GW = 2048
GM = GW // P
FF = 4096
FM = FF // P
EPS = 1e-5
ALPHA = float((2 * 2) ** 0.25)
QK_SCALE = float(HD) ** -0.5
MASKED = -3.0e38
LNS = 4
PIECES = 4
PW = D // PIECES
EVENTS = NT * PIECES
IN_ORDER = [(t, q) for q in range(PIECES) for t in range(NT)]
LN_ORDER = [(0, 0), (0, 1), (1, 0), (1, 1), (0, 2), (1, 2), (0, 3), (1, 3)]
OUT_ORDER = [(t, q) for t in range(NT) for q in range(PIECES)]


def pieces_in(order, q):
    return 1 + max(order.index((t, p)) for t in range(NT) for p in range(q + 1))


UNIT = 2048
HALF = UNIT // 2
SLOTS = 4
LOOK = 6
N_PROJ, N_OUT, N_FF, N_GV, N_GU, N_GO = 14, 4, 16, 8, 8, 8
U_PROJ = 0
U_OUT = U_PROJ + N_PROJ
U_FA = U_OUT + N_OUT
U_FB = U_FA + N_FF
U_GV = U_FB + N_FF
U_GU = U_GV + N_GV
U_GO = U_GU + N_GU
U_FC = U_GO + N_GO
U_FD = U_FC + N_FF
UNITS = U_FD + N_FF

QB, KB, VB, QA, KA, VA, GA = range(7)
GROUP_COLUMN = [4 * RW, 5 * RW, 6 * RW, 0, RW, 2 * RW, 3 * RW]
ROTATED = (QB, KB, QA, KA)


def split_bits(value, bits, parts):
    out, rest = [], float(value)
    for n in range(parts):
        if n == parts - 1:
            out.append(float(np.float32(rest)))
        else:
            e = np.floor(np.log2(abs(rest)))
            step = 2.0 ** (e - bits + 1)
            out.append(float(np.trunc(rest / step) * step))
        rest -= out[-1]
        if rest == 0.0:
            break
    return out


class Count:

    def __init__(self, eng, sem):
        self.eng, self.sem, self.n = eng, sem, 0

    def inc(self, ins):
        ins.then_inc(self.sem, 1)
        self.n += 1
        return self.n

    def wait(self, n=None):
        self.eng.wait_ge(self.sem, self.n if n is None else n)


def build(nc, x, positions, ln_gain, ln_bias, mix_w_in, ret_gn_gain, mix_w_out, gmlp_w_uv,
          gmlp_b_uv, gmlp_ln_gain, gmlp_ln_bias, gmlp_w_s, gmlp_b_s, gmlp_w_out, ffn_w_in,
          ffn_w_out, inv_freq, decay, out):
    ctx = ExitStack()
    with ctx:
        def sb(name, shape, dt=F32):
            return ctx.enter_context(nc.sbuf_tensor(name, shape, dt))

        def sem(name):
            return ctx.enter_context(nc.semaphore(name))

        raw = sb("raw", [P, SLOTS, UNIT])
        w_high = sb("w_high", [P, SLOTS, UNIT], F32R)
        w_low = sb("w_low", [P, SLOTS, UNIT], F32R)
        xt_high = sb("xt_high", [P, KD, SEQ], F32R)
        xt_low = sb("xt_low", [P, KD, SEQ], F32R)
        ht_high = sb("ht_high", [P, 4, SEQ], F32R)
        ht_low = sb("ht_low", [P, 4, SEQ], F32R)
        resid = sb("resid", [P, NT, D])
        work = sb("work", [P, NT, D])
        ident = sb("ident", [P, P])
        ones = sb("ones", [P, P])
        small = sb("small", [P, 512])
        arena = sb("arena", [P, 16384])

        def area(start, *shape):
            n = int(np.prod(shape))
            v = arena[:, start:start + n]
            if len(shape) == 2:
                return v.rearrange("p (a b) -> p a b", a=shape[0])
            return v

        qk_t = {g: area(1024 * i, HEAD_PAIRS, SEQ) for i, g in enumerate(ROTATED)}
        qk_n = [area(4096 + 1024 * i, NT, RW) for i in range(2)]
        v_n = {VB: area(6144, NT, RW), VA: area(0, NT, RW)}
        gate = area(1024, NT, RW)
        y_moba, y_ret = qk_n
        p_moba = area(7168, HEADS, 3 * P)
        p_ret = area(10240, HEADS, 3 * P)
        decay_t = area(13312, HEADS, SEQ)
        causal = area(15360, 3 * P)
        gn_gain = area(15744, RW)
        hidden = area(0, FM, SEQ)
        v_gate = area(4096, NT, GW)
        spatial_add = area(8192, GM, P)
        v_bias = area(10240, GW)
        b_s_all = area(10240, GROUPS, P)
        ws_t = area(12288, GROUPS, P)
        ln_tab = area(13312, 2, D)
        ws_n = area(15360, GROUPS, P)

        cos2 = sb("cos2", [P, NT, HD])
        sin2 = sb("sin2", [P, NT, HD])
        ang = sb("ang", [P, NT, ROPE_HALF])
        turns = sb("turns", [P, NT, ROPE_HALF])
        freq = sb("freq", [P, ROPE_HALF])
        pos_i = sb("pos_i", [P, NT], I32)
        rows48 = sb("rows48", [3 * GM, P])
        cols48 = sb("cols48", [P, 3 * GM])
        vn_tile = work[:, 0, 0:512].rearrange("p (s t c) -> p s t c", s=2, t=NT)
        mixed = work[:, 0, 512:1024].rearrange("p (s c) -> p s c", s=2)
        u_tile = work[:, 1, :].rearrange("p (s c) -> p s c", s=4)

        used_cols = [0]

        def cols(n):
            a = used_cols[0]
            used_cols[0] += n
            return small[:, a:a + n]

        pos_f = cols(NT)
        mx = cols(2 * HEADS)
        neg_mx = cols(2 * HEADS)
        p_sum = cols(2 * HEADS)
        p_inv = cols(2 * HEADS)
        gn_stats = cols(6 * 2 * HEADS)
        gn_mv = cols(2 * 2 * HEADS)
        gn_rstd = cols(2 * HEADS)
        ln_stats = cols(6 * 2 * NT)
        ln_mv = cols(2 * NT)
        ln_rstd = cols(NT)
        v_stats = cols(6 * 4 * NT)
        v_mv = cols(2 * NT)
        v_rstd = cols(NT)
        half_pi = cols(1)

        ps_y = ctx.enter_context(nc.psum_tensor("ps_y", [P, 4, 512], F32))
        ps_m = ctx.enter_context(nc.psum_tensor("ps_m", [P, 4, 512], F32))

        raw_landed = [sem(f"raw_landed{i}") for i in range(2 * SLOTS)]
        w_high_ready = sem("w_high_ready")
        w_low_ready = sem("w_low_ready")
        w_used = sem("w_used")
        x_landed = [sem(f"x_landed{q}") for q in range(PIECES)]
        rope_in_landed = sem("rope_in_landed")
        freq_landed = sem("freq_landed")
        decay_landed = sem("decay_landed")
        gain_landed = sem("gain_landed")
        tab_landed = sem("tab_landed")
        tab2_landed = sem("tab2_landed")
        ws_landed = sem("ws_landed")
        rows_landed = [sem(f"rows_landed{i}") for i in range(3)]
        bs_landed = sem("bs_landed")
        vb_landed = sem("vb_landed")
        out_written = [sem(f"out_written{i}") for i in range(4)]
        consts_ready = sem("consts_ready")
        pool_step = sem("pool_step")
        ones_ready = sem("ones_ready")
        dve_step = sem("dve_step")
        half_pi_ready = sem("half_pi_ready")
        angles_ready = sem("angles_ready")
        abs_ready = sem("abs_ready")
        rope_tab_ready = sem("rope_tab_ready")
        xt_turned = sem("xt_turned")
        xt_high_ready = sem("xt_high_ready")
        xt_low_ready = sem("xt_low_ready")
        rope_products = sem("rope_products")
        rope_added = sem("rope_added")
        qk_turned = sem("qk_turned")
        qk_t_ready = sem("qk_t_ready")
        moba_scores = sem("moba_scores")
        moba_masked = sem("moba_masked")
        moba_max = sem("moba_max")
        moba_exp = sem("moba_exp")
        p_turned = sem("p_turned")
        p_t_ready = sem("p_t_ready")
        ret_scores = sem("ret_scores")
        ret_decayed = sem("ret_decayed")
        v_ready = sem("v_ready")
        moba_out = sem("moba_out")
        ret_out = sem("ret_out")
        y_moba_ready = sem("y_moba_ready")
        y_ret_ready = sem("y_ret_ready")
        gate_silu = sem("gate_silu")
        gate_ready = sem("gate_ready")
        gn_centred = sem("gn_centred")
        gn_var = sem("gn_var")
        gn_std = sem("gn_std")
        c_turned = sem("c_turned")
        c_high_ready = sem("c_high_ready")
        c_low_ready = sem("c_low_ready")
        y_done = sem("y_done")
        ln_var = sem("ln_var")
        ln_std = sem("ln_std")
        ln_done = sem("ln_done")
        act_out = sem("act_out")
        hidden_ready = sem("hidden_ready")
        ht_high_ready = sem("ht_high_ready")
        ht_low_ready = sem("ht_low_ready")
        ws_masked = sem("ws_masked")
        ws_turned = sem("ws_turned")
        ws_t_ready = sem("ws_t_ready")
        row_sums = sem("row_sums")
        spatial_add_ready = sem("spatial_add_ready")
        v_biased = sem("v_biased")
        v_gelu = sem("v_gelu")
        v_stat = sem("v_stat")
        v_var = sem("v_var")
        v_std = sem("v_std")
        vn_ready = sem("vn_ready")
        spatial_done = sem("spatial_done")
        mixed_ready = sem("mixed_ready")

        x_v = x[0].rearrange("(t p) d -> p t d", p=P)
        out_v = out[0].rearrange("(t p) d -> p t d", p=P)
        w_in_v = mix_w_in[0].rearrange("(k p) n -> p k n", p=P)
        w_out_v = mix_w_out[0].rearrange("(k p) n -> p k n", p=P)
        w_uv_v = gmlp_w_uv[0].rearrange("(k p) n -> p k n", p=P)
        w_go_v = gmlp_w_out[0].rearrange("(k p) n -> p k n", p=P)
        w1_v = [ffn_w_in[l].rearrange("(k p) n -> p k n", p=P) for l in range(2)]
        w2_v = [ffn_w_out[l].rearrange("(k p) n -> p k n", p=P) for l in range(2)]

        def wide(tile, slot):
            return tile[:, slot, :].rearrange("p (k n) -> p k n", k=4)

        def tall(tile, slot, half):
            return tile[:, slot, half * HALF:(half + 1) * HALF].rearrange("p (k c) -> p k c", k=KD)

        def flat(tile, slot, half):
            return tile[:, slot, half * HALF:(half + 1) * HALF]

        TURN_BANKS = [ps_m[:, 3, 0:PW]] + [ps_y[:, b, 0:PW] for b in range(4)]

        def piece_bank(e):
            return TURN_BANKS[e % len(TURN_BANKS)].rearrange("p (k c) -> p k c", k=2)

        def split_high(act, unit_base, j, i=0):
            u, h = unit_base + j // 2, j % 2
            half = 2 * unit_base + j
            act.wait_ge(raw_landed[half % (2 * SLOTS)], 16 * (u // SLOTS + 1 + i))
            if half >= 2 * SLOTS:
                act.wait_ge(w_used, half - 2 * SLOTS + 1 + 8 * i)
            nc.scalar.activation(flat(w_high, u % SLOTS, h), flat(raw, u % SLOTS, h),
                                 ACT.Copy).then_inc(w_high_ready, 1)

        def split_low(dve, unit_base, j, i=0):
            u, h = unit_base + j // 2, j % 2
            dve.wait_ge(w_high_ready, 2 * unit_base + j + 1 + 8 * i)
            nc.vector.tensor_tensor(flat(w_low, u % SLOTS, h), flat(raw, u % SLOTS, h),
                                    flat(w_high, u % SLOTS, h), ALU.subtract).then_inc(w_low_ready, 1)

        total_halves = 2 * UNITS

        def ahead(step, eng, unit_base, j, i=0):
            half = 2 * unit_base + j + LOOK
            if isinstance(i, int):
                half, i = half + 8 * i, 0
            if half < total_halves:
                step(eng, half // 2, half % 2, i)

        block = ctx.enter_context(nc.Block())

        @block.sync
        def _(sp):
            def load(half, i, src):
                if half >= 2 * SLOTS:
                    sp.wait_ge(w_low_ready, half - 2 * SLOTS + 1 + 8 * i)
                dst = flat(raw, half // 2 % SLOTS, half % 2)
                if len(src.shape) == 3:
                    dst = dst.rearrange("p (k n) -> p k n", k=src.shape[1])
                sp.dma_start(dst, src).then_inc(raw_landed[half % (2 * SLOTS)], 16)

            def load_tall(view, unit_base, n):
                with sp.Fori(0, n // 4) as i:
                    for j in range(8):
                        load(2 * unit_base + j, i, view[:, :, bass.ds((8 * i + j) * P, P)])

            def load_rows(view, unit_base, n):
                with sp.Fori(0, n // 4) as i:
                    for j in range(8):
                        load(2 * unit_base + j, i, view[:, bass.ds(8 * i + j, 1), :])

            def load_tables(ln):
                if ln == 0:
                    sp.wait_ge(ret_decayed, HEADS)
                else:
                    sp.wait_ge(ln_done, EVENTS * ln)
                sp.dma_start(ln_tab[:, 0, :], ln_gain[ln // 2, ln % 2].partition_broadcast(P)) \
                  .then_inc(tab_landed, 16)
                sp.dma_start(ln_tab[:, 1, :], ln_bias[ln // 2, ln % 2].partition_broadcast(P)) \
                  .then_inc(tab2_landed, 16)

            for j in range(2 * N_PROJ):
                if j < PIECES:
                    s = slice(j * PW, (j + 1) * PW)
                    sp.dma_start(resid[:, :, s], x_v[:, :, s]).then_inc(x_landed[j], 16)
                c = GROUP_COLUMN[j // 4]
                load(j, 0, w_in_v[:, 2 * (j % 4):2 * (j % 4) + 2, c:c + RW])
                if j == 7:
                    sp.dma_start(decay_t, decay.rearrange("p (h i) -> p h i", h=HEADS)) \
                      .then_inc(decay_landed, 16)
                    sp.dma_start(gn_gain, ret_gn_gain[0].partition_broadcast(P)) \
                      .then_inc(gain_landed, 16)
            for j in range(2 * N_OUT):
                k = (4 + j) % KD
                load(2 * U_OUT + j, 0, w_out_v[:, k, :])
            load_tables(0)
            sp.wait_ge(gate_ready, NT)
            sp.wait_ge(moba_masked, HEADS)
            sp.dma_start(ws_n, gmlp_w_s[0].rearrange("g i j -> i g j")).then_inc(ws_landed, 16)
            sp.dma_start(rows48[0:GM, :], gmlp_b_uv[0, 0:GW].rearrange("(m c) -> m c", m=GM)) \
              .then_inc(rows_landed[0], 16)
            sp.dma_start(rows48[GM:2 * GM, :], gmlp_ln_gain[0].rearrange("(m c) -> m c", m=GM)) \
              .then_inc(rows_landed[1], 16)
            sp.dma_start(rows48[2 * GM:3 * GM, :], gmlp_ln_bias[0].rearrange("(m c) -> m c", m=GM)) \
              .then_inc(rows_landed[2], 16)
            sp.wait_ge(ret_out, 1)
            sp.dma_start(b_s_all, gmlp_b_s[0].partition_broadcast(P)).then_inc(bs_landed, 16)
            load_tall(w1_v[0], U_FA, N_FF)
            load_tables(1)
            load_rows(w2_v[0], U_FB, N_FF)
            sp.wait_ge(spatial_add_ready, GM)
            sp.dma_start(v_bias, gmlp_b_uv[0, GW:2 * GW].partition_broadcast(P)).then_inc(vb_landed, 16)
            with sp.Fori(0, N_GV // 4) as i:
                for j in range(8):
                    c = GW + (2 * i + j // 4) * RW
                    load(2 * U_GV + j, i, w_uv_v[:, 2 * (j % 4):2 * (j % 4) + 2, bass.ds(c, RW)])
            load_tables(2)
            load_tall(w_uv_v, U_GU, N_GU)
            load_rows(w_go_v, U_GO, N_GO)
            load_tall(w1_v[1], U_FC, N_FF)
            load_tables(3)
            load_rows(w2_v[1], U_FD, N_FF)
            for t in range(NT):
                for n in range(2):
                    sp.wait_ge(ln_done, EVENTS * (LNS - 1) + OUT_ORDER.index((t, 2 * n + 1)) + 1)
                    s = slice(n * HALF_D, (n + 1) * HALF_D)
                    sp.dma_start(out_v[:, t, s], resid[:, t, s]).then_inc(out_written[2 * t + n], 16)
            for s in out_written:
                sp.wait_ge(s, 16)

        @block.gpsimd
        def _(pool):
            step = Count(pool, pool_step)
            pool.dma_start(pos_i[:, :], positions.rearrange("a (t p) -> p (a t)", p=P),
                           allow_slow_non_contiguous=True) \
                .then_inc(rope_in_landed, 16)
            pool.dma_start(freq[:, :], inv_freq.partition_broadcast(P)).then_inc(freq_landed, 16)
            step.inc(nc.gpsimd.memset(ident[:, :], 0.0))
            step.inc(nc.gpsimd.memset(causal, 0.0))
            nc.gpsimd.memset(ones[:, :], 1.0).then_inc(ones_ready, 1)
            nc.gpsimd.memset(half_pi, float(np.pi / 2)).then_inc(half_pi_ready, 1)
            step.wait()
            nc.gpsimd.affine_select(out=ident[:, :], in_=ident[:, :], compare_op=ALU.not_equal,
                                    fill=1.0, base=0, pattern=[[-1, P]], channel_multiplier=1) \
                .then_inc(consts_ready, 1)
            lower = causal[:, P:3 * P]
            nc.gpsimd.affine_select(out=lower, in_=lower, compare_op=ALU.is_ge, fill=MASKED, base=0,
                                    pattern=[[0, 2], [-1, P]], channel_multiplier=1) \
                .then_inc(consts_ready, 1)

            def angle_part(n):
                w = NT * ROPE_HALF
                return work[:, 0, n * w:(n + 1) * w].rearrange("p (t f) -> p t f", t=NT)

            def angles():
                pool.wait_ge(rope_in_landed, 16)
                step.inc(nc.gpsimd.tensor_copy(pos_f, pos_i[:, :]))
                pool.wait_ge(freq_landed, 16)
                step.wait()
                for t in range(NT):
                    step.inc(nc.gpsimd.tensor_scalar(ang[:, t, :], freq[:, :], pos_f[:, t:t + 1], None, ALU.mult))
                step.wait()
                magic = 1.5 * 2.0 ** 23
                for level, parts in ((24, 6), (12, 5), (0, 4)):
                    period = 2.0 * np.pi * 2.0 ** level
                    step.inc(nc.gpsimd.tensor_scalar(turns[:, :, :], ang[:, :, :], float(1.0 / period), magic,
                                                     ALU.mult, ALU.add))
                    step.wait()
                    step.inc(nc.gpsimd.tensor_scalar(turns[:, :, :], turns[:, :, :], magic, None, ALU.subtract))
                    step.wait()
                    period_parts = split_bits(period, 11, parts)
                    made = [step.inc(nc.gpsimd.tensor_scalar(angle_part(n), turns[:, :, :], part, None, ALU.mult))
                            for n, part in enumerate(period_parts)]
                    for n in range(len(period_parts)):
                        step.wait(made[n] if n == 0 else None)
                        step.inc(nc.gpsimd.tensor_tensor(ang[:, :, :], ang[:, :, :], angle_part(n), ALU.subtract))
                    step.wait()
                pi_below = 3.1415925
                nc.gpsimd.tensor_scalar(ang[:, :, :], ang[:, :, :], pi_below, -pi_below, ALU.min, ALU.max) \
                    .then_inc(angles_ready, 1)

            angles()

            for r in range(len(ROTATED)):
                for t in range(NT):
                    pool.wait_ge(rope_products, 3 * (NT * r + t) + 3)
                    if r >= 2:
                        pool.wait_ge(qk_turned, NT * (r - 2) + t + 1)
                    nc.gpsimd.tensor_tensor(qk_n[r % 2][:, t, :], work[:, t, 0:RW],
                                            work[:, t, RW:2 * RW], ALU.add).then_inc(rope_added, 1)

            pool.wait_ge(gain_landed, 16)
            for t in range(NT):
                pool.wait_ge(gate_silu, t + 1)
                nc.gpsimd.tensor_tensor(gate[:, t, :], gate[:, t, :], gn_gain, ALU.mult) \
                    .then_inc(gate_ready, 1)

            def squares(tile_base):
                with pool.Fori(0, FM // 8) as i:
                    for j in range(8):
                        pool.wait_ge(act_out, tile_base + 8 * i + j + 1)
                        h = hidden[:, bass.ds(8 * i + j, 1), :]
                        nc.gpsimd.tensor_tensor(h, h, h, ALU.mult).then_inc(hidden_ready, 1)

            pool.wait_ge(ws_landed, 16)
            nc.gpsimd.affine_select(out=ws_n, in_=ws_n, compare_op=ALU.is_ge, fill=0.0, base=0,
                                    pattern=[[0, GROUPS], [-1, P]], channel_multiplier=1) \
                .then_inc(ws_masked, 1)
            squares(0)
            with pool.Fori(0, GM // 8) as i:
                for j in range(8):
                    pool.wait_ge(act_out, FM + 8 * i + j + 1)
                    pool.wait_ge(mixed_ready, 8 * i + j + 1)
                    nc.gpsimd.tensor_tensor(hidden[:, bass.ds(8 * i + j, 1), :],
                                            mixed[:, j % 2:j % 2 + 1, :], u_tile[:, j % 4:j % 4 + 1, :],
                                            ALU.mult).then_inc(hidden_ready, 1)
            squares(FM + GM)

        @block.scalar
        def _(act):
            def ln_scalar(ln, t):
                act.wait_ge(ln_var, NT * ln + t + 1)
                nc.scalar.activation(ln_rstd[:, t:t + 1], ln_rstd[:, t:t + 1], ACT.Sqrt) \
                    .then_inc(ln_std, 1)

            def xt_piece(turned, e, order):
                t, q = order[e]
                act.wait_ge(xt_turned, turned + e + 1)
                nc.scalar.activation(xt_high[:, 2 * q:2 * q + 2, t * P:(t + 1) * P], piece_bank(e),
                                     ACT.Copy).then_inc(xt_high_ready, 1)

            def qk_out(g):
                for t in range(NT):
                    act.wait_ge(qk_turned, NT * ROTATED.index(g) + t + 1)
                    nc.scalar.activation(qk_t[g][:, :, t * P:(t + 1) * P],
                                         ps_m[:, 2 * (g % 2) + t, :].rearrange("p (k c) -> p k c", k=4),
                                         ACT.Copy).then_inc(qk_t_ready, 1)

            def v_out(g):
                act.wait_ge(w_used, 4 * (g + 1))
                for t in range(NT):
                    nc.scalar.activation(v_n[g][:, t, :], ps_m[:, 2 * (g % 2) + t, :],
                                         ACT.Copy).then_inc(v_ready, 1)

            def exps(batch):
                act.wait_ge(moba_max, batch + 1)
                for h in range(4 * batch, 4 * batch + 4):
                    for t, s in ((1, slice(0, 2 * P)), (0, slice(2 * P, 3 * P))):
                        c = t * HEADS + h
                        nc.scalar.activation(p_moba[:, h, s], p_moba[:, h, s], ACT.Exp,
                                             bias=neg_mx[:, c:c + 1], scale=QK_SCALE,
                                             accum_out=p_sum[:, c:c + 1]).then_inc(moba_exp, 1)

            def p_out(h):
                act.wait_ge(p_turned, h + 1)
                nc.scalar.activation(p_moba[:, h, :], ps_y[:, h % 2, 0:3 * P], ACT.Copy) \
                    .then_inc(p_t_ready, 1)

            for j, q in ((0, 0), (1, 1), (2, None), (3, 2), (4, 3), (5, None)):
                if q is not None:
                    for t in range(NT):
                        xt_piece(0, NT * q + t, IN_ORDER)
                split_high(act, 0, j)

            for j in range(2 * N_PROJ):
                ahead(split_high, act, 0, j)
                if j == 1:
                    act.wait_ge(angles_ready, 1)
                    act.wait_ge(half_pi_ready, 1)
                    nc.scalar.activation(turns[:, :, :], ang[:, :, :], ACT.Abs).then_inc(abs_ready, 1)
                    nc.scalar.activation(sin2[:, :, 0:ROPE_HALF], ang[:, :, :], ACT.Sin, scale=-1.0) \
                        .then_inc(rope_tab_ready, 1)
                    nc.scalar.activation(sin2[:, :, ROPE_HALF:HD], ang[:, :, :], ACT.Sin) \
                        .then_inc(rope_tab_ready, 1)
                    act.wait_ge(abs_ready, 1)
                    for s in (slice(0, ROPE_HALF), slice(ROPE_HALF, HD)):
                        nc.scalar.activation(cos2[:, :, s], turns[:, :, :], ACT.Sin, bias=half_pi,
                                             scale=-1.0).then_inc(rope_tab_ready, 1)
                if j in (6, 10, 18, 22):
                    qk_out((QB, KB, None, QA, KA)[(j - 6) // 4])
                if j == 12:
                    v_out(VB)
                if j == 13:
                    exps(0)
                if j == 15:
                    exps(1)
                if 16 <= j < 20:
                    for h in (2 * (j - 16), 2 * (j - 16) + 1):
                        p_out(h)
                if j == 22:
                    for t in range(NT):
                        act.wait_ge(c_turned, t + 1)
                        nc.scalar.activation(ht_high[:, :, t * P:(t + 1) * P],
                                             ps_y[:, t, :].rearrange("p (k c) -> p k c", k=4), ACT.Copy) \
                            .then_inc(c_high_ready, 1)
                if j == 24:
                    v_out(VA)
            act.wait_ge(gn_var, 1)
            nc.scalar.activation(gn_rstd, gn_rstd, ACT.Sqrt).then_inc(gn_std, 1)
            act.wait_ge(w_used, 4 * (GA + 1))
            for t in range(NT):
                nc.scalar.activation(gate[:, t, :], ps_m[:, 2 * (GA % 2) + t, :], ACT.Silu) \
                    .then_inc(gate_silu, 1)
            for j in range(4):
                ahead(split_high, act, U_OUT, j)
            for t in range(NT):
                act.wait_ge(c_turned, NT + t + 1)
                nc.scalar.activation(xt_high[:, 0:4, t * P:(t + 1) * P],
                                     ps_m[:, 2 + t, :].rearrange("p (k c) -> p k c", k=4), ACT.Copy) \
                    .then_inc(c_high_ready, 1)

            def tail(ln, unit_base):
                ahead(split_high, act, unit_base, 0)
                ln_scalar(ln, 0)
                if ln == LNS - 1:
                    ln_scalar(ln, 1)
                    return
                for e in range(EVENTS):
                    if LN_ORDER[e] == (1, 0):
                        ln_scalar(ln, 1)
                    xt_piece(EVENTS * (ln + 1), e, LN_ORDER)
                for j in range(1, 4):
                    ahead(split_high, act, unit_base, j)

            tail(0, U_OUT + 2)

            def tall_stage(unit_base, n, tile_base, finish, ready, after_first=None):
                def tile(i, j):
                    ahead(split_high, act, unit_base, j, i)
                    if isinstance(i, int) and 8 * i + j == 2 * n - 1:
                        for k in range(2):
                            hidden_high(k, ready, 2 * (unit_base + n))
                    act.wait_ge(w_used, 2 * unit_base + 8 * i + j + 1)
                    finish(i, j, ps_m[:, j % 4, 0:SEQ]).then_inc(act_out, 1)

                bodies = n // 4
                first = 0
                if after_first is not None:
                    for j in range(8):
                        tile(0, j)
                    after_first()
                    first = 1
                with act.Fori(first, bodies - 1) as i:
                    for j in range(8):
                        tile(i, j)
                for j in range(8):
                    tile(bodies - 1, j)

            def relu_tile(i, j, bank):
                return nc.scalar.activation(hidden[:, bass.ds(8 * i + j, 1), :].rearrange("p a b -> p (a b)"),
                                            bank, ACT.Relu)

            def hidden_high(n, ready, half, i=0):
                act.wait_ge(hidden_ready, ready + n + 1 + 8 * i)
                act.wait_ge(w_used, half + n - 4 + 1 + 8 * i)
                src = hidden[:, n, :] if isinstance(i, int) and i == 0 else \
                    hidden[:, bass.ds(8 * i + n, 1), :].rearrange("p a b -> p (a b)")
                nc.scalar.activation(ht_high[:, n % 4, :], src, ACT.Copy).then_inc(ht_high_ready, 1)

            def rows_stage(ln, unit_base, tiles, ready):
                loops = (tiles - 4) // 8
                if loops > 1:
                    with act.Fori(0, loops) as i:
                        for j in range(8):
                            ahead(split_high, act, unit_base, j, i)
                            hidden_high(j + 2, ready, 2 * unit_base, i)
                for n in range(8 * loops if loops > 1 else 0, tiles - 4):
                    ahead(split_high, act, unit_base, n)
                    hidden_high(n + 2, ready, 2 * unit_base)
                for n in range(tiles - 2, tiles):
                    hidden_high(n, ready, 2 * unit_base)
                tail(ln, unit_base + tiles // 2 - 2)

            def small_tables():
                act.wait_ge(ws_turned, 3)
                nc.scalar.activation(cols48[:, :], ps_y[:, 2, 0:3 * GM], ACT.Copy).then_inc(ws_t_ready, 1)
                for b in range(2):
                    nc.scalar.activation(ws_t[:, 4 * b:4 * b + 4, :],
                                         ps_y[:, b, :].rearrange("p (g c) -> p g c", g=4),
                                         ACT.Copy).then_inc(ws_t_ready, 1)

            tall_stage(U_FA, N_FF, 0, relu_tile, 0, small_tables)
            rows_stage(1, U_FB, FM, 0)

            with act.Fori(0, N_GV // 4) as i:
                for j in range(8):
                    ahead(split_high, act, U_GV, j, i)
                    if j % 4 == 3:
                        for t in range(NT):
                            act.wait_ge(v_biased, 4 * i + 2 * (j // 4) + t + 1)
                            v = v_gate[:, t, bass.ds((2 * i + j // 4) * RW, RW)]
                            nc.scalar.activation(v, v, ACT.Gelu_apprx_tanh).then_inc(v_gelu, 1)
            act.wait_ge(v_var, 1)
            nc.scalar.activation(v_rstd, v_rstd, ACT.Sqrt).then_inc(v_std, 1)
            for j in range(2 * N_GU):
                ahead(split_high, act, U_GU, j)
                if j == 2 * N_GU - 1:
                    for k in range(2):
                        hidden_high(k, FM, 2 * U_GO)
                act.wait_ge(w_used, 2 * U_GU + j + 1)
                if j >= 4:
                    act.wait_ge(hidden_ready, FM + j - 3)
                nc.scalar.activation(u_tile[:, j % 4, :], ps_m[:, j % 4, 0:SEQ], ACT.Gelu_apprx_tanh,
                                     bias=cols48[:, j:j + 1]).then_inc(act_out, 1)
            rows_stage(2, U_GO, GM, FM)
            tall_stage(U_FC, N_FF, FM + GM, relu_tile, FM + GM)
            rows_stage(3, U_FD, FM, FM + GM)

        @block.vector
        def _(dve):
            step = Count(dve, dve_step)
            def xt_piece(turned, e, order):
                t, q = order[e]
                dve.wait_ge(xt_high_ready, turned + e + 1)
                s = (slice(None), slice(2 * q, 2 * q + 2), slice(t * P, (t + 1) * P))
                nc.vector.tensor_tensor(xt_low[s], piece_bank(e), xt_high[s], ALU.subtract) \
                    .then_inc(xt_low_ready, 1)

            def rstd_of(var, out_cols):
                step.inc(nc.vector.tensor_scalar(out_cols, var, EPS, None, ALU.add))
                step.wait()
                return nc.vector.reciprocal(out_cols, out_cols)

            def add_resid(ln, t, n, end):
                if (t, n) == (1, 1):
                    dve.wait_ge(w_used, end)
                else:
                    dve.wait_ge(y_done, 3 * ln + 2 * t + n + 1)
                s = slice(n * HALF_D, (n + 1) * HALF_D)
                step.inc(nc.vector.scalar_tensor_tensor(
                    out=work[:, t, s], in0=resid[:, t, s], scalar=ALPHA, in1=ps_y[:, 2 * t + n, :],
                    op0=ALU.mult, op1=ALU.add))
                step.wait()
                c = 6 * (2 * t + n)
                step.inc(nc.vector.bn_stats(ln_stats[:, c:c + 6], work[:, t, s]))

            def variance(ln, t):
                step.wait()
                mv = ln_mv[:, 2 * t:2 * t + 2]
                step.inc(nc.vector.bn_aggr(mv, ln_stats[:, 12 * t:12 * t + 12]))
                step.wait()
                rstd_of(mv[:, 1:2], ln_rstd[:, t:t + 1]).then_inc(ln_var, 1)

            def ln_piece(ln, e, order):
                t, q = order[e]
                s = slice(q * PW, (q + 1) * PW)
                step.inc(nc.vector.scalar_tensor_tensor(
                    out=work[:, t, s], in0=work[:, t, s], scalar=ln_mv[:, 2 * t:2 * t + 1],
                    in1=ln_tab[:, 0, s], op0=ALU.subtract, op1=ALU.mult))
                dve.wait_ge(ln_std, NT * ln + t + 1)
                step.wait()
                nc.vector.scalar_tensor_tensor(out=resid[:, t, s], in0=work[:, t, s],
                                               scalar=ln_rstd[:, t:t + 1], in1=ln_tab[:, 1, s],
                                               op0=ALU.mult, op1=ALU.add).then_inc(ln_done, 1)

            def layer_norm(ln, end):
                last = ln == LNS - 1
                order = OUT_ORDER if last else LN_ORDER
                for n in range(2):
                    add_resid(ln, 0, n, end)
                variance(ln, 0)
                dve.wait_ge(tab_landed, 16 * (ln + 1))
                dve.wait_ge(tab2_landed, 16 * (ln + 1))
                first = order.index((1, 0))
                for e in range(first):
                    ln_piece(ln, e, order)
                add_resid(ln, 1, 0, end)
                if not last:
                    xt_piece(EVENTS * (ln + 1), 0, order)
                add_resid(ln, 1, 1, end)
                variance(ln, 1)
                for e in range(first, EVENTS):
                    ln_piece(ln, e, order)
                    if not last:
                        xt_piece(EVENTS * (ln + 1), e - 1, order)
                if not last:
                    xt_piece(EVENTS * (ln + 1), EVENTS - 1, order)

            for j, q in ((0, 0), (1, 1), (2, None), (3, 2), (4, 3), (5, None)):
                if q is not None:
                    for t in range(NT):
                        xt_piece(0, NT * q + t, IN_ORDER)
                split_low(dve, 0, j)

            def rope(g):
                dve.wait_ge(w_used, 4 * (g + 1))
                r = ROTATED.index(g)
                if r == 0:
                    dve.wait_ge(rope_tab_ready, 4)
                for t in range(NT):
                    if r > 0:
                        dve.wait_ge(rope_added, NT * (r - 1) + t + 1)
                    src = ps_m[:, 2 * (g % 2) + t, :].rearrange("p (h d) -> p h d", h=HEADS)
                    a = work[:, t, 0:RW].rearrange("p (h d) -> p h d", h=HEADS)
                    b = work[:, t, RW:2 * RW].rearrange("p (h d) -> p h d", h=HEADS)
                    wide_cos = cos2[:, t:t + 1, :].to_broadcast([P, HEADS, HD])
                    wide_sin = sin2[:, t:t + 1, :].to_broadcast([P, HEADS, HD])
                    nc.vector.tensor_tensor(a, src, wide_cos, ALU.mult).then_inc(rope_products, 1)
                    for to, of in ((slice(0, ROPE_HALF), slice(ROPE_HALF, HD)),
                                   (slice(ROPE_HALF, HD), slice(0, ROPE_HALF))):
                        nc.vector.tensor_tensor(b[:, :, to], src[:, :, of], wide_sin[:, :, to],
                                                ALU.mult).then_inc(rope_products, 1)

            def moba_mask(batch):
                if batch == 0:
                    dve.wait_ge(consts_ready, 2)
                for h in range(4 * batch, 4 * batch + 4):
                    dve.wait_ge(moba_scores, h + 1)
                    nc.vector.tensor_tensor(p_moba[:, h, :], ps_y[:, h % 4, 0:3 * P], causal,
                                            ALU.add).then_inc(moba_masked, 1)
                hs = slice(4 * batch, 4 * batch + 4)
                dve.wait_ge(moba_masked, 4 * batch + 4)
                for t, s in ((1, slice(0, 2 * P)), (0, slice(2 * P, 3 * P))):
                    step.inc(nc.vector.tensor_reduce(mx[:, t * HEADS:(t + 1) * HEADS][:, hs], p_moba[:, hs, s],
                                                     AX_X, ALU.max))
                step.wait()
                two = lambda c: c.rearrange("p (t h) -> p t h", t=2)[:, :, hs]
                nc.vector.tensor_scalar(two(neg_mx), two(mx), -QK_SCALE, None, ALU.mult).then_inc(moba_max, 1)

            def ret_decay(batch):
                if batch == 0:
                    dve.wait_ge(decay_landed, 16)
                for h in range(4 * batch, 4 * batch + 4):
                    dve.wait_ge(ret_scores, h + 1)
                    nc.vector.tensor_tensor(p_ret[:, h, 0:2 * P], ps_y[:, h % 4, 0:2 * P],
                                            decay_t[:, h, :], ALU.mult)
                    nc.vector.tensor_tensor(p_ret[:, h, 2 * P:3 * P], ps_y[:, h % 4, 2 * P:3 * P],
                                            decay_t[:, h, 0:P], ALU.mult).then_inc(ret_decayed, 1)

            def per_head(c):
                return c.unsqueeze(2).to_broadcast([P, HEADS, HD])

            def moba_output():
                dve.wait_ge(moba_exp, 2 * HEADS)
                step.inc(nc.vector.reciprocal(p_inv, p_sum))
                step.wait()
                dve.wait_ge(moba_out, 1)
                for t in range(NT):
                    nc.vector.tensor_tensor(y_moba[:, t, :].rearrange("p (h d) -> p h d", h=HEADS),
                                            ps_y[:, 2 + t, :].rearrange("p (h d) -> p h d", h=HEADS),
                                            per_head(p_inv[:, t * HEADS:(t + 1) * HEADS]),
                                            ALU.mult).then_inc(y_moba_ready, 1)

            gn_pairs = gn_mv.rearrange("p (c two) -> p c two", two=2)

            def group_statistics():
                dve.wait_ge(ret_out, 1)
                for t in range(NT):
                    for h in range(HEADS):
                        c = 6 * (t * HEADS + h)
                        step.inc(nc.vector.bn_stats(gn_stats[:, c:c + 6], ps_m[:, 2 + t, h * HD:(h + 1) * HD]))
                step.wait()
                for c in range(2 * HEADS):
                    step.inc(nc.vector.bn_aggr(gn_mv[:, 2 * c:2 * c + 2], gn_stats[:, 6 * c:6 * c + 6]))
                step.wait()
                rstd_of(gn_pairs[:, :, 1], gn_rstd).then_inc(gn_var, 1)

            def group_norm():
                for t in range(NT):
                    y = y_ret[:, t, :].rearrange("p (h d) -> p h d", h=HEADS)
                    s = slice(t * HEADS, (t + 1) * HEADS)
                    step.inc(nc.vector.tensor_tensor(y, ps_m[:, 2 + t, :].rearrange("p (h d) -> p h d", h=HEADS),
                                                     per_head(gn_pairs[:, s, 0]), ALU.subtract))
                dve.wait_ge(gn_std, 1)
                step.wait()
                for t in range(NT):
                    y = y_ret[:, t, :].rearrange("p (h d) -> p h d", h=HEADS)
                    step.inc(nc.vector.tensor_tensor(y, y, per_head(gn_rstd[:, t * HEADS:(t + 1) * HEADS]),
                                                     ALU.mult))
                step.wait()

            for j in range(2 * N_PROJ):
                ahead(split_low, dve, 0, j)
                if j in (4, 8, 16, 20):
                    rope(j // 4 - 1)
                if j == 12:
                    moba_mask(0)
                if j == 14:
                    moba_mask(1)
                if j == 20:
                    moba_output()
                if j == 22:
                    for t in range(NT):
                        dve.wait_ge(c_high_ready, t + 1)
                        nc.vector.tensor_tensor(ht_low[:, :, t * P:(t + 1) * P],
                                                ps_y[:, t, :].rearrange("p (k c) -> p k c", k=4),
                                                ht_high[:, :, t * P:(t + 1) * P], ALU.subtract) \
                            .then_inc(c_low_ready, 1)
                if j == 24:
                    ret_decay(0)
                if j == 25:
                    ret_decay(1)
                if j == 26:
                    group_statistics()
            group_norm()
            for t in range(NT):
                dve.wait_ge(gate_ready, t + 1)
                nc.vector.tensor_tensor(y_ret[:, t, :], y_ret[:, t, :], gate[:, t, :],
                                        ALU.mult).then_inc(y_ret_ready, 1)
            for j in range(4):
                ahead(split_low, dve, U_OUT, j)
            for t in range(NT):
                dve.wait_ge(c_high_ready, NT + t + 1)
                nc.vector.tensor_tensor(xt_low[:, 0:4, t * P:(t + 1) * P],
                                        ps_m[:, 2 + t, :].rearrange("p (k c) -> p k c", k=4),
                                        xt_high[:, 0:4, t * P:(t + 1) * P], ALU.subtract) \
                    .then_inc(c_low_ready, 1)

            def tail(ln, unit_base):
                ahead(split_low, dve, unit_base, 0)
                layer_norm(ln, 2 * unit_base + 4)
                for j in range(1, 4):
                    ahead(split_low, dve, unit_base, j)

            tail(0, U_OUT + 2)

            def tall_stage(unit_base, n):
                with dve.Fori(0, n // 4) as i:
                    for j in range(8):
                        ahead(split_low, dve, unit_base, j, i)

            def hidden_low(n, seen, i=0):
                dve.wait_ge(ht_high_ready, seen + n + 1 + 8 * i)
                src = hidden[:, n, :] if isinstance(i, int) and i == 0 else \
                    hidden[:, bass.ds(8 * i + n, 1), :].rearrange("p a b -> p (a b)")
                nc.vector.tensor_tensor(ht_low[:, n % 4, :], src, ht_high[:, n % 4, :], ALU.subtract) \
                    .then_inc(ht_low_ready, 1)

            def rows_stage(ln, unit_base, tiles, seen, between=None):
                for n in range(2):
                    hidden_low(n, seen)
                loops = (tiles - 4) // 8
                if loops > 1:
                    with dve.Fori(0, loops) as i:
                        for j in range(8):
                            ahead(split_low, dve, unit_base, j, i)
                            hidden_low(j + 2, seen, i)
                if between is not None:
                    between()
                for n in range(8 * loops if loops > 1 else 0, tiles - 4):
                    ahead(split_low, dve, unit_base, n)
                    hidden_low(n + 2, seen)
                for n in range(tiles - 2, tiles):
                    hidden_low(n, seen)
                tail(ln, unit_base + tiles // 2 - 2)

            def spatial_table():
                dve.wait_ge(row_sums, 2)
                dve.wait_ge(bs_landed, 16)
                dve.wait_ge(ws_t_ready, 3)
                for m in range(GM):
                    g = m // 2
                    bank = 3 if g < 4 else 0
                    nc.vector.scalar_tensor_tensor(out=spatial_add[:, m, :],
                                                   in0=ps_m[:, bank, (g % 4) * P:(g % 4 + 1) * P],
                                                   scalar=cols48[:, 2 * GM + m:2 * GM + m + 1],
                                                   in1=b_s_all[:, g, :], op0=ALU.mult, op1=ALU.add) \
                        .then_inc(spatial_add_ready, 1)

            tall_stage(U_FA, N_FF)
            rows_stage(1, U_FB, FM, 0, spatial_table)

            dve.wait_ge(vb_landed, 16)
            with dve.Fori(0, N_GV // 4) as i:
                for j in range(8):
                    ahead(split_low, dve, U_GV, j, i)
                    if j % 4 == 3:
                        g = j // 4
                        dve.wait_ge(w_used, 2 * U_GV + 8 * i + j + 1)
                        for t in range(NT):
                            nc.vector.tensor_tensor(v_gate[:, t, bass.ds((2 * i + g) * RW, RW)],
                                                    ps_m[:, 2 * g + t, :], v_bias[:, bass.ds((2 * i + g) * RW, RW)],
                                                    ALU.add).then_inc(v_biased, 1)
                        for t in range(NT):
                            dve.wait_ge(v_gelu, 4 * i + 2 * g + t + 1)
                            nc.vector.bn_stats(v_stats[:, bass.ds(24 * t + 6 * (2 * i + g), 6)],
                                               v_gate[:, t, bass.ds((2 * i + g) * RW, RW)]).then_inc(v_stat, 1)
            dve.wait_ge(v_stat, 4 * NT)
            for t in range(NT):
                step.inc(nc.vector.bn_aggr(v_mv[:, 2 * t:2 * t + 2], v_stats[:, 24 * t:24 * t + 24]))
            step.wait()
            rstd_of(v_mv.rearrange("p (t two) -> p t two", two=2)[:, :, 1], v_rstd).then_inc(v_var, 1)
            dve.wait_ge(v_std, 1)

            def normalise(m, i):
                for t in range(NT):
                    nc.vector.tensor_scalar(vn_tile[:, m % 2, t, :], v_gate[:, t, bass.ds((8 * i + m) * P, P)],
                                            v_mv[:, 2 * t:2 * t + 1], v_rstd[:, t:t + 1],
                                            ALU.subtract, ALU.mult).then_inc(vn_ready, 1)

            def mix(m, i):
                dve.wait_ge(spatial_done, m + 1 + 8 * i)
                dve.wait_ge(hidden_ready, FM - 1 + m + 8 * i)
                tile = bass.ds(8 * i + m, 1)
                nc.vector.scalar_tensor_tensor(
                    out=mixed[:, m % 2, :].rearrange("p (t c) -> p t c", t=NT),
                    in0=ps_y[:, m % 4, 0:SEQ].rearrange("p (t c) -> p t c", t=NT),
                    scalar=cols48[:, bass.ds(8 * i + (GM + m), 1)],
                    in1=spatial_add[:, tile, :].to_broadcast([P, NT, P]),
                    op0=ALU.mult, op1=ALU.add).then_inc(mixed_ready, 1)

            dve.wait_ge(spatial_add_ready, GM)
            with dve.Fori(0, N_GU // 4) as i:
                for j in range(8):
                    normalise(j, i)
                    ahead(split_low, dve, U_GU, j, i)
                    mix(j, i)
            rows_stage(2, U_GO, GM, FM)
            tall_stage(U_FC, N_FF)
            rows_stage(3, U_FD, FM, FM + GM)

        @block.tensor
        def _(pe):
            def turn(bank, src, n=4):
                for c in range(n):
                    last = nc.tensor.transpose(bank[:, c * P:(c + 1) * P], src[:, c * P:(c + 1) * P], ident[:, :])
                return last

            def turn_piece(turned, e, order):
                t, q = order[e]
                if e >= len(TURN_BANKS):
                    pe.wait_ge(xt_low_ready, turned + e - len(TURN_BANKS) + 1)
                turn(TURN_BANKS[e % len(TURN_BANKS)], resid[:, t, q * PW:(q + 1) * PW], 2) \
                    .then_inc(xt_turned, 1)

            def turn_ln(ln, e):
                pe.wait_ge(ln_done, EVENTS * ln + e + 1)
                turn_piece(EVENTS * (ln + 1), e, LN_ORDER)

            def wide_half(slot, quarter, banks):
                hi, lo = wide(w_high, slot), wide(w_low, slot)
                for k in (2 * quarter, 2 * quarter + 1):
                    k4 = k % 4
                    for t in range(NT):
                        s = slice(t * P, (t + 1) * P)
                        out_b = banks[t]
                        nc.tensor.matmul(out_b, xt_high[:, k, s], hi[:, k4, :], start=(k == 0), stop=False)
                        nc.tensor.matmul(out_b, xt_high[:, k, s], lo[:, k4, :], start=False, stop=False)
                        mm = nc.tensor.matmul(out_b, xt_low[:, k, s], hi[:, k4, :], start=False,
                                              stop=(k == KD - 1))
                return mm

            def turn_input(q):
                pe.wait_ge(x_landed[q], 16)
                for t in range(NT):
                    turn_piece(0, NT * q + t, IN_ORDER)

            pe.wait_ge(consts_ready, 1)
            turn_input(0)
            turn_input(1)

            def turn_qk(g):
                r = ROTATED.index(g)
                for t in range(NT):
                    pe.wait_ge(rope_added, NT * r + t + 1)
                    turn(ps_m[:, 2 * (g % 2) + t, :], qk_n[r % 2][:, t, :]).then_inc(qk_turned, 1)

            def scores_moba(pair):
                for h in (2 * pair, 2 * pair + 1):
                    rows = slice((h % 2) * HD, (h % 2 + 1) * HD)
                    if h >= 4:
                        pe.wait_ge(moba_masked, h - 3)
                    q, k = qk_t[QB][rows, pair, :], qk_t[KB][rows, pair, :]
                    bank = ps_y[:, h % 4, :]
                    nc.tensor.matmul(bank[:, 0:2 * P], q[:, P:2 * P], k[:, 0:2 * P], start=True, stop=True)
                    nc.tensor.matmul(bank[:, 2 * P:3 * P], q[:, 0:P], k[:, 0:P], start=True, stop=True) \
                        .then_inc(moba_scores, 1)

            def scores_ret(pair):
                for h in (2 * pair, 2 * pair + 1):
                    rows = slice((h % 2) * HD, (h % 2 + 1) * HD)
                    if h >= 4:
                        pe.wait_ge(ret_decayed, h - 3)
                    q, k = qk_t[QA][rows, pair, :], qk_t[KA][rows, pair, :]
                    bank = ps_y[:, h % 4, :]
                    nc.tensor.matmul(bank[:, 0:2 * P], k[:, 0:P], q[:, 0:2 * P], start=True, stop=True)
                    nc.tensor.matmul(bank[:, 2 * P:3 * P], k[:, P:2 * P], q[:, P:2 * P], start=True, stop=True) \
                        .then_inc(ret_scores, 1)

            def turn_p(h):
                pe.wait_ge(moba_exp, 2 * h + 2)
                if h < 2:
                    pe.wait_ge(moba_masked, HEADS - 2)
                else:
                    pe.wait_ge(p_t_ready, h - 1)
                turn(ps_y[:, h % 2, :], p_moba[:, h, :], 3).then_inc(p_turned, 1)

            def values_moba():
                pe.wait_ge(v_ready, NT)
                pe.wait_ge(moba_masked, HEADS)
                for h in range(HEADS):
                    pe.wait_ge(p_t_ready, h + 1)
                    c = slice(h * HD, (h + 1) * HD)
                    w = p_moba[:, h, :]
                    nc.tensor.matmul(ps_y[:, 3, c], w[:, 0:P], v_n[VB][:, 0, c], start=True, stop=False)
                    nc.tensor.matmul(ps_y[:, 3, c], w[:, P:2 * P], v_n[VB][:, 1, c], start=False, stop=True)
                    mm = nc.tensor.matmul(ps_y[:, 2, c], w[:, 2 * P:3 * P], v_n[VB][:, 0, c],
                                          start=True, stop=True)
                mm.then_inc(moba_out, 1)

            def values_ret():
                pe.wait_ge(v_ready, 2 * NT)
                for h in range(HEADS):
                    pe.wait_ge(ret_decayed, h + 1)
                    c = slice(h * HD, (h + 1) * HD)
                    w = p_ret[:, h, :]
                    nc.tensor.matmul(ps_m[:, 2, c], w[:, 0:P], v_n[VA][:, 0, c], start=True, stop=True)
                    nc.tensor.matmul(ps_m[:, 3, c], w[:, P:2 * P], v_n[VA][:, 0, c], start=True, stop=False)
                    mm = nc.tensor.matmul(ps_m[:, 3, c], w[:, 2 * P:3 * P], v_n[VA][:, 1, c],
                                          start=False, stop=True)
                mm.then_inc(ret_out, 1)

            def turn_moba_output():
                for t in range(NT):
                    pe.wait_ge(y_moba_ready, t + 1)
                    turn(ps_y[:, t, :], y_moba[:, t, :]).then_inc(c_turned, 1)

            pair_read = {VB: (qk_t_ready, NT), QA: (qk_t_ready, 2 * NT), KA: (v_ready, NT),
                         VA: (qk_t_ready, 3 * NT), GA: (qk_t_ready, 4 * NT)}
            for j in range(2 * N_PROJ):
                g, q = j // 4, j % 4
                if q == 0 and g in pair_read:
                    pe.wait_ge(*pair_read[g])
                if g == 0:
                    if q in (1, 2):
                        turn_input(q + 1)
                    pe.wait_ge(xt_low_ready, pieces_in(IN_ORDER, q))
                pe.wait_ge(w_low_ready, j + 1)
                wide_half((j // 2) % SLOTS, q, [ps_m[:, 2 * (g % 2) + t, :] for t in range(NT)]) \
                    .then_inc(w_used, 1)
                if j in (5, 9, 17, 21):
                    turn_qk((QB, KB, None, QA, KA)[(j - 5) // 4])
                if j == 11:
                    pe.wait_ge(qk_t_ready, 2 * NT)
                    scores_moba(0)
                    scores_moba(1)
                if j == 13:
                    scores_moba(2)
                    scores_moba(3)
                if 15 <= j < 19:
                    turn_p(2 * (j - 15))
                    turn_p(2 * (j - 15) + 1)
                if j == 19:
                    values_moba()
                if j == 21:
                    turn_moba_output()
                if j == 23:
                    pe.wait_ge(qk_t_ready, 4 * NT)
                    pe.wait_ge(c_low_ready, NT)
                    scores_ret(0)
                    scores_ret(1)
                if j == 24:
                    scores_ret(2)
                    scores_ret(3)
                if j == 25:
                    values_ret()

            def rows_products(stationary, t, n, slot, half, start, stop):
                (hi, lo) = stationary
                s = slice(t * P, (t + 1) * P)
                c = slice(n * HALF_D, (n + 1) * HALF_D)
                bank = ps_y[:, 2 * t + n, :]
                wh, wl = flat(w_high, slot, half)[:, c], flat(w_low, slot, half)[:, c]
                nc.tensor.matmul(bank, hi[:, s], wh, start=start, stop=False)
                nc.tensor.matmul(bank, hi[:, s], wl, start=False, stop=False)
                return nc.tensor.matmul(bank, lo[:, s], wh, start=False, stop=stop)

            def rows_half(unit_base, j, stationary, start):
                for t in range(NT):
                    for n in range(2):
                        mm = rows_products(stationary, t, n, (unit_base + j // 2) % SLOTS, j % 2, start, False)
                mm.then_inc(w_used, 1)

            def rows_tail(unit_base, stationary, ready):
                for t in range(NT):
                    for n in range(2):
                        for j in range(4):
                            if t == 0 and n == 0:
                                pe.wait_ge(w_low_ready, 2 * unit_base + j + 1)
                                ready(j)
                            mm = rows_products(stationary(j), t, n, (unit_base + j // 2) % SLOTS, j % 2,
                                               False, j == 3)
                            if (t, n) == (1, 1):
                                mm.then_inc(w_used, 1)
                        if (t, n) != (1, 1):
                            mm.then_inc(y_done, 1)

            pe.wait_ge(ret_decayed, HEADS)
            for j in range(4):
                pe.wait_ge(w_low_ready, 2 * U_OUT + j + 1)
                rows_half(U_OUT, j, (ht_high[:, j, :], ht_low[:, j, :]), j == 0)
            for t in range(NT):
                pe.wait_ge(y_ret_ready, t + 1)
                turn(ps_m[:, 2 + t, :], y_ret[:, t, :]).then_inc(c_turned, 1)
            pe.wait_ge(c_low_ready, 2 * NT)
            rows_tail(U_OUT + 2, lambda j: (xt_high[:, j, :], xt_low[:, j, :]), lambda j: None)

            def tall_products(slot, half, bank, ks=range(KD)):
                hi, lo = tall(w_high, slot, half), tall(w_low, slot, half)
                for k in ks:
                    nc.tensor.matmul(bank, hi[:, k, :], xt_high[:, k, :], start=(k == 0), stop=False)
                    nc.tensor.matmul(bank, hi[:, k, :], xt_low[:, k, :], start=False, stop=False)
                    mm = nc.tensor.matmul(bank, lo[:, k, :], xt_high[:, k, :], start=False, stop=(k == KD - 1))
                return mm

            def tall_stage(unit_base, n, tile_base, ln, after_first=None):
                def tile(i, j):
                    pe.wait_ge(w_low_ready, 2 * unit_base + 8 * i + j + 1)
                    if not (isinstance(i, int) and tile_base + 8 * i + j < 4):
                        pe.wait_ge(act_out, tile_base + 8 * i + j - 3)
                    tall_products((unit_base + j // 2) % SLOTS, j % 2, ps_m[:, j % 4, 0:SEQ]) \
                        .then_inc(w_used, 1)

                turn_between = {(0, 1): 4, (0, 2): 5, (1, 1): 6, (2, 0): 7}
                for e in range(4):
                    turn_ln(ln, e)
                pe.wait_ge(w_low_ready, 2 * unit_base + 3)
                for q in range(PIECES):
                    pe.wait_ge(xt_low_ready, EVENTS * (ln + 1) + pieces_in(LN_ORDER, q))
                    for j in range(3):
                        mm = tall_products((unit_base + j // 2) % SLOTS, j % 2, ps_m[:, j, 0:SEQ],
                                           (2 * q, 2 * q + 1))
                        if q == PIECES - 1:
                            mm.then_inc(w_used, 1)
                        if (q, j) in turn_between:
                            turn_ln(ln, turn_between[q, j])
                for j in range(3, 8):
                    tile(0, j)
                if after_first is not None:
                    after_first()
                with pe.Fori(1, n // 4) as i:
                    for j in range(8):
                        tile(i, j)

            def rows_stage(unit_base, tiles, seen, between=None):
                def ready(j, i=0):
                    pe.wait_ge(ht_low_ready, seen + j + 1 + 8 * i)

                for j in range(4):
                    pe.wait_ge(w_low_ready, 2 * unit_base + j + 1)
                    ready(j)
                    rows_half(unit_base, j, (ht_high[:, j, :], ht_low[:, j, :]), j == 0)
                if between is not None:
                    between()
                loops = (tiles - 8) // 8
                if loops > 1:
                    with pe.Fori(0, loops) as i:
                        for j in range(4, 12):
                            pe.wait_ge(w_low_ready, 2 * unit_base + 8 * i + j + 1)
                            ready(j, i)
                            rows_half(unit_base, j, (ht_high[:, j % 4, :], ht_low[:, j % 4, :]), False)
                for j in range(4 + (8 * loops if loops > 1 else 0), tiles - 4):
                    pe.wait_ge(w_low_ready, 2 * unit_base + j + 1)
                    ready(j)
                    rows_half(unit_base, j, (ht_high[:, j % 4, :], ht_low[:, j % 4, :]), False)
                rows_tail(unit_base + tiles // 2 - 2, lambda j: (ht_high[:, j, :], ht_low[:, j, :]),
                          lambda j: ready(tiles - 4 + j))

            def row_sum_products():
                pe.wait_ge(ones_ready, 1)
                pe.wait_ge(ws_t_ready, 3)
                for b, bank in ((0, 3), (1, 0)):
                    nc.tensor.matmul(ps_m[:, bank, :], ones[:, :],
                                     ws_t[:, 4 * b:4 * b + 4, :].rearrange("p g c -> p (g c)"),
                                     start=True, stop=True).then_inc(row_sums, 1)

            def turn_small():
                pe.wait_ge(ws_masked, 1)
                for b in range(2):
                    turn(ps_y[:, b, :], ws_n[:, 4 * b:4 * b + 4, :].rearrange("p g c -> p (g c)")) \
                        .then_inc(ws_turned, 1)
                for s in rows_landed:
                    pe.wait_ge(s, 16)
                nc.tensor.transpose(ps_y[:, 2, 0:3 * GM], rows48[:, :], ident[0:3 * GM, 0:3 * GM]) \
                    .then_inc(ws_turned, 1)

            tall_stage(U_FA, N_FF, 0, 0, turn_small)
            pe.wait_ge(act_out, FM)
            pe.wait_ge(ws_t_ready, 3)
            rows_stage(U_FB, FM, 0, row_sum_products)
            pe.wait_ge(spatial_add_ready, GM)
            for e in range(4):
                turn_ln(1, e)

            for j in range(2 * N_GV):
                g, q = j // 4, j % 4
                if g == 0:
                    if q in (1, 2):
                        turn_ln(1, 2 + 2 * q)
                        turn_ln(1, 3 + 2 * q)
                    pe.wait_ge(xt_low_ready, 2 * EVENTS + pieces_in(LN_ORDER, q))
                if q == 0 and g >= 2:
                    pe.wait_ge(v_biased, NT * (g - 1))
                pe.wait_ge(w_low_ready, 2 * U_GV + j + 1)
                wide_half((U_GV + j // 2) % SLOTS, q, [ps_m[:, 2 * (g % 2) + t, :] for t in range(NT)]) \
                    .then_inc(w_used, 1)

            def mix_tile(m):
                pe.wait_ge(vn_ready, 2 * m + 2)
                if m >= 4:
                    pe.wait_ge(mixed_ready, m - 3)
                for t in range(NT):
                    mm = nc.tensor.matmul(ps_y[:, m % 4, t * P:(t + 1) * P], vn_tile[:, m % 2, t, :],
                                          ws_t[:, m // 2, :], start=True, stop=True)
                mm.then_inc(spatial_done, 1)

            lag = 2
            for m in range(GM + lag):
                if m < GM:
                    pe.wait_ge(w_low_ready, 2 * U_GU + m + 1)
                    if m in (0, 2):
                        pe.wait_ge(v_biased, (3 if m == 0 else 4) * NT)
                    if m >= 4:
                        pe.wait_ge(act_out, FM + m - 3)
                    tall_products((U_GU + m // 2) % SLOTS, m % 2, ps_m[:, m % 4, 0:SEQ]) \
                        .then_inc(w_used, 1)
                if m >= lag:
                    mix_tile(m - lag)
            pe.wait_ge(mixed_ready, GM)
            pe.wait_ge(act_out, FM + GM)
            rows_stage(U_GO, GM, FM)

            tall_stage(U_FC, N_FF, FM + GM, 2)
            rows_stage(U_FD, FM, FM + GM)


_INS = ["x", "positions", "ln_gain", "ln_bias", "mix_w_in", "ret_gn_gain", "mix_w_out", "gmlp_w_uv",
        "gmlp_b_uv", "gmlp_ln_gain", "gmlp_ln_bias", "gmlp_w_s", "gmlp_b_s", "gmlp_w_out", "ffn_w_in",
        "ffn_w_out"]


def shape_constants():
    freq = (10000.0 ** (-np.arange(0, HD, 2) / HD)).astype(np.float32)
    gamma = 1.0 - 2.0 ** (-5.0 - np.arange(HEADS))
    diff = np.arange(SEQ)[None, None, :] - np.arange(P)[:, None, None]
    decay = np.where(diff >= 0, gamma[None, :, None] ** np.maximum(diff, 0), 0.0) * QK_SCALE
    return freq, decay.astype(np.float32).reshape(P, HEADS * SEQ)


def kernel(**inputs):
    import concourse.bacc as bacc
    from concourse.bass_utils import run_bass_kernel_spmd

    nc = bacc.Bacc("TRN2", target_bir_lowering=False, num_devices=1)
    arrays = {name: np.ascontiguousarray(inputs[name]) for name in _INS}
    arrays["inv_freq"], arrays["decay"] = shape_constants()
    args = [nc.dram_tensor(f"in_{name}", a.shape, mybir.dt.from_np(a.dtype), kind="ExternalInput").ap()
            for name, a in arrays.items()]
    args.append(nc.dram_tensor("out_0", (1, SEQ, D), F32, kind="ExternalOutput").ap())
    build(nc, *args)
    r = run_bass_kernel_spmd(nc, [{f"in_{name}": a for name, a in arrays.items()}], core_ids=[0])
    return r.results[0]["out_0"]
```

```python
from contextlib import ExitStack

import numpy as np

import concourse.bass as bass
from concourse import mybir

F32 = mybir.dt.float32
F32R = mybir.dt.float32r
I32 = mybir.dt.int32
ALU = mybir.AluOpType
ACT = mybir.ActivationFunctionType
AX_X = mybir.AxisListType.X

P = 128
SEQ = 256
NT = SEQ // P
D = 1024
KD = D // P
HALF_D = D // 2
HEADS = 8
HD = 64
HEAD_PAIRS = HEADS // 2
ROPE_HALF = HD // 2
RW = HEADS * HD
GROUPS = 8
GW = 2048
GM = GW // P
FF = 4096
FM = FF // P
EPS = 1e-5
ALPHA = float((2 * 2) ** 0.25)
QK_SCALE = float(HD) ** -0.5
MASKED = -3.0e38
LNS = 4
PIECES = 4
PW = D // PIECES
EVENTS = NT * PIECES
IN_ORDER = [(t, q) for q in range(PIECES) for t in range(NT)]
LN_ORDER = [(0, 0), (0, 1), (1, 0), (1, 1), (0, 2), (1, 2), (0, 3), (1, 3)]
OUT_ORDER = [(t, q) for t in range(NT) for q in range(PIECES)]
LN_ORDERS = [LN_ORDER, OUT_ORDER, LN_ORDER, OUT_ORDER]
SPLIT_FIRST = [1, 2, 1, 1]
Y_BLOCKS = [(0, 0, 512), (0, 512, 512), (1, 0, 512), (1, 512, 256), (1, 768, 256)]
LAST_BLOCK = len(Y_BLOCKS) - 1


def pieces_in(order, q):
    return 1 + max(order.index((t, p)) for t in range(NT) for p in range(q + 1))


UNIT = 2048
HALF = UNIT // 2
SLOTS = 4
LOOK = 6
N_PROJ, N_OUT, N_FF, N_GV, N_GU, N_GO = 14, 4, 16, 8, 8, 8
U_PROJ = 0
U_OUT = U_PROJ + N_PROJ
U_FA = U_OUT + N_OUT
U_FB = U_FA + N_FF
U_GV = U_FB + N_FF
U_GU = U_GV + N_GV
U_GO = U_GU + N_GU
U_FC = U_GO + N_GO
U_FD = U_FC + N_FF
UNITS = U_FD + N_FF

QB, KB, VB, QA, KA, VA, GA = range(7)
GROUP_COLUMN = [4 * RW, 5 * RW, 6 * RW, 0, RW, 2 * RW, 3 * RW]
ROTATED = (QB, KB, QA, KA)


def split_bits(value, bits, parts):
    out, rest = [], float(value)
    for n in range(parts):
        if n == parts - 1:
            out.append(float(np.float32(rest)))
        else:
            e = np.floor(np.log2(abs(rest)))
            step = 2.0 ** (e - bits + 1)
            out.append(float(np.trunc(rest / step) * step))
        rest -= out[-1]
        if rest == 0.0:
            break
    return out


class Count:

    def __init__(self, eng, sem):
        self.eng, self.sem, self.n = eng, sem, 0

    def inc(self, ins):
        ins.then_inc(self.sem, 1)
        self.n += 1
        return self.n

    def wait(self, n=None):
        self.eng.wait_ge(self.sem, self.n if n is None else n)


def build(nc, x, positions, ln_gain, ln_bias, mix_w_in, ret_gn_gain, mix_w_out, gmlp_w_uv,
          gmlp_b_uv, gmlp_ln_gain, gmlp_ln_bias, gmlp_w_s, gmlp_b_s, gmlp_w_out, ffn_w_in,
          ffn_w_out, inv_freq, decay, out):
    ctx = ExitStack()
    with ctx:
        def sb(name, shape, dt=F32):
            return ctx.enter_context(nc.sbuf_tensor(name, shape, dt))

        def sem(name):
            return ctx.enter_context(nc.semaphore(name))

        raw = sb("raw", [P, SLOTS, UNIT])
        w_high = sb("w_high", [P, SLOTS, UNIT], F32R)
        w_low = sb("w_low", [P, SLOTS, UNIT], F32R)
        xt_high = sb("xt_high", [P, KD, SEQ], F32R)
        xt_low = sb("xt_low", [P, KD, SEQ], F32R)
        ht_high = sb("ht_high", [P, 4, SEQ], F32R)
        ht_low = sb("ht_low", [P, 4, SEQ], F32R)
        resid = sb("resid", [P, NT, D])
        work = sb("work", [P, NT, D])
        ident = sb("ident", [P, P])
        ones = sb("ones", [P, P])
        small = sb("small", [P, 512])
        arena = sb("arena", [P, 16384])

        def area(start, *shape):
            n = int(np.prod(shape))
            v = arena[:, start:start + n]
            if len(shape) == 2:
                return v.rearrange("p (a b) -> p a b", a=shape[0])
            return v

        qk_t = {g: area(1024 * i, HEAD_PAIRS, SEQ) for i, g in enumerate(ROTATED)}
        qk_n = [area(4096 + 1024 * i, NT, RW) for i in range(2)]
        v_n = {VB: area(6144, NT, RW), VA: area(0, NT, RW)}
        gate = area(1024, NT, RW)
        y_moba, y_ret = qk_n
        p_moba = area(7168, HEADS, 3 * P)
        p_ret = area(10240, HEADS, 3 * P)
        decay_t = area(13312, HEADS, SEQ)
        causal = area(15360, 3 * P)
        gn_gain = area(15744, RW)
        hidden = area(0, FM, SEQ)
        v_gate = area(4096, NT, GW)
        spatial_add = area(8192, GM, P)
        v_bias = area(10240, GW)
        b_s_all = area(10240, GROUPS, P)
        ws_t = area(12288, GROUPS, P)
        ln_tab = area(13312, 2, D)
        ws_n = area(15360, GROUPS, P)

        cos2 = sb("cos2", [P, NT, HD])
        sin2 = sb("sin2", [P, NT, HD])
        ang = sb("ang", [P, NT, ROPE_HALF])
        turns = sb("turns", [P, NT, ROPE_HALF])
        freq = sb("freq", [P, ROPE_HALF])
        pos_i = sb("pos_i", [P, NT], I32)
        rows48 = sb("rows48", [3 * GM, P])
        cols48 = sb("cols48", [P, 3 * GM])
        vn_tile = work[:, 0, 0:512].rearrange("p (s t c) -> p s t c", s=2, t=NT)
        mixed = work[:, 0, 512:1024].rearrange("p (s c) -> p s c", s=2)
        u_tile = work[:, 1, :].rearrange("p (s c) -> p s c", s=4)

        used_cols = [0]

        def cols(n):
            a = used_cols[0]
            used_cols[0] += n
            return small[:, a:a + n]

        pos_f = cols(NT)
        mx = cols(2 * HEADS)
        neg_mx = cols(2 * HEADS)
        p_sum = cols(2 * HEADS)
        p_inv = cols(2 * HEADS)
        gn_stats = cols(6 * 2 * HEADS)
        gn_mv = cols(2 * 2 * HEADS)
        gn_rstd = cols(2 * HEADS)
        ln_stats = cols(6 * 4 * NT)
        ln_mv = cols(2 * NT)
        ln_rstd = cols(NT)
        v_stats = cols(6 * 4 * NT)
        v_mv = cols(2 * NT)
        v_rstd = cols(NT)
        half_pi = cols(1)

        ps_y = ctx.enter_context(nc.psum_tensor("ps_y", [P, 4, 512], F32))
        ps_m = ctx.enter_context(nc.psum_tensor("ps_m", [P, 4, 512], F32))

        def y_bank(b):
            return ps_m[:, 1, 0:Y_BLOCKS[b][2]] if b == LAST_BLOCK else ps_y[:, b, 0:Y_BLOCKS[b][2]]

        raw_landed = [sem(f"raw_landed{i}") for i in range(2 * SLOTS)]
        w_high_ready = sem("w_high_ready")
        w_low_ready = sem("w_low_ready")
        w_used = sem("w_used")
        x_landed = [sem(f"x_landed{q}") for q in range(PIECES)]
        rope_in_landed = sem("rope_in_landed")
        freq_landed = sem("freq_landed")
        decay_landed = sem("decay_landed")
        gain_landed = sem("gain_landed")
        tab_landed = sem("tab_landed")
        tab2_landed = sem("tab2_landed")
        ws_landed = sem("ws_landed")
        rows_landed = [sem(f"rows_landed{i}") for i in range(3)]
        bs_landed = sem("bs_landed")
        vb_landed = sem("vb_landed")
        out_written = [sem(f"out_written{i}") for i in range(4)]
        consts_ready = sem("consts_ready")
        pool_step = sem("pool_step")
        ones_ready = sem("ones_ready")
        dve_step = sem("dve_step")
        half_pi_ready = sem("half_pi_ready")
        angles_ready = sem("angles_ready")
        abs_ready = sem("abs_ready")
        rope_tab_ready = sem("rope_tab_ready")
        xt_turned = sem("xt_turned")
        xt_high_ready = sem("xt_high_ready")
        xt_low_ready = sem("xt_low_ready")
        rope_products = sem("rope_products")
        rope_added = sem("rope_added")
        qk_turned = sem("qk_turned")
        qk_t_ready = sem("qk_t_ready")
        moba_scores = sem("moba_scores")
        moba_masked = sem("moba_masked")
        moba_max = sem("moba_max")
        moba_exp = sem("moba_exp")
        p_turned = sem("p_turned")
        p_t_ready = sem("p_t_ready")
        ret_scores = sem("ret_scores")
        ret_decayed = sem("ret_decayed")
        v_ready = sem("v_ready")
        moba_out = sem("moba_out")
        ret_out = sem("ret_out")
        y_moba_ready = sem("y_moba_ready")
        y_ret_ready = sem("y_ret_ready")
        gate_silu = sem("gate_silu")
        gate_ready = sem("gate_ready")
        gn_centred = sem("gn_centred")
        gn_var = sem("gn_var")
        gn_std = sem("gn_std")
        c_turned = sem("c_turned")
        c_high_ready = sem("c_high_ready")
        c_low_ready = sem("c_low_ready")
        y_done = sem("y_done")
        ln_var = sem("ln_var")
        ln_std = sem("ln_std")
        ln_done = sem("ln_done")
        act_out = sem("act_out")
        hidden_ready = sem("hidden_ready")
        ht_high_ready = sem("ht_high_ready")
        ht_low_ready = sem("ht_low_ready")
        ws_masked = sem("ws_masked")
        ws_turned = sem("ws_turned")
        ws_t_ready = sem("ws_t_ready")
        row_sums = sem("row_sums")
        spatial_add_ready = sem("spatial_add_ready")
        v_biased = sem("v_biased")
        v_gelu = sem("v_gelu")
        v_stat = sem("v_stat")
        v_var = sem("v_var")
        v_std = sem("v_std")
        vn_ready = sem("vn_ready")
        spatial_done = sem("spatial_done")
        mixed_ready = sem("mixed_ready")

        x_v = x[0].rearrange("(t p) d -> p t d", p=P)
        out_v = out[0].rearrange("(t p) d -> p t d", p=P)
        w_in_v = mix_w_in[0].rearrange("(k p) n -> p k n", p=P)
        w_out_v = mix_w_out[0].rearrange("(k p) n -> p k n", p=P)
        w_uv_v = gmlp_w_uv[0].rearrange("(k p) n -> p k n", p=P)
        w_go_v = gmlp_w_out[0].rearrange("(k p) n -> p k n", p=P)
        w1_v = [ffn_w_in[l].rearrange("(k p) n -> p k n", p=P) for l in range(2)]
        w2_v = [ffn_w_out[l].rearrange("(k p) n -> p k n", p=P) for l in range(2)]

        def wide(tile, slot):
            return tile[:, slot, :].rearrange("p (k n) -> p k n", k=4)

        def tall(tile, slot, half):
            return tile[:, slot, half * HALF:(half + 1) * HALF].rearrange("p (k c) -> p k c", k=KD)

        def flat(tile, slot, half):
            return tile[:, slot, half * HALF:(half + 1) * HALF]

        TURNS = 5

        def piece_bank(order, e):
            banks = ((ps_m, 3), (ps_y, 0), (ps_y, 1), (ps_y, 2), (ps_y, 3))
            if order is OUT_ORDER:
                banks = ((ps_m, 3), (ps_y, 0), (ps_y, 1), (ps_m, 2), (ps_y, 2))
            tile, bank = banks[e % TURNS]
            return tile[:, bank, 0:PW]

        def piece_tiles(order, e):
            return piece_bank(order, e).rearrange("p (k c) -> p k c", k=2)

        def split_high(act, unit_base, j, i=0):
            u, h = unit_base + j // 2, j % 2
            half = 2 * unit_base + j
            act.wait_ge(raw_landed[half % (2 * SLOTS)], 16 * (u // SLOTS + 1 + i))
            if half >= 2 * SLOTS:
                act.wait_ge(w_used, half - 2 * SLOTS + 1 + 8 * i)
            nc.scalar.activation(flat(w_high, u % SLOTS, h), flat(raw, u % SLOTS, h),
                                 ACT.Copy).then_inc(w_high_ready, 1)

        def split_low(dve, unit_base, j, i=0):
            u, h = unit_base + j // 2, j % 2
            dve.wait_ge(w_high_ready, 2 * unit_base + j + 1 + 8 * i)
            nc.vector.tensor_tensor(flat(w_low, u % SLOTS, h), flat(raw, u % SLOTS, h),
                                    flat(w_high, u % SLOTS, h), ALU.subtract).then_inc(w_low_ready, 1)

        total_halves = 2 * UNITS

        def ahead(step, eng, unit_base, j, i=0):
            half = 2 * unit_base + j + LOOK
            if isinstance(i, int):
                half, i = half + 8 * i, 0
            if half < total_halves:
                step(eng, half // 2, half % 2, i)

        block = ctx.enter_context(nc.Block())

        @block.sync
        def _(sp):
            def load(half, i, src):
                if half >= 2 * SLOTS:
                    sp.wait_ge(w_low_ready, half - 2 * SLOTS + 1 + 8 * i)
                dst = flat(raw, half // 2 % SLOTS, half % 2)
                if len(src.shape) == 3:
                    dst = dst.rearrange("p (k n) -> p k n", k=src.shape[1])
                sp.dma_start(dst, src).then_inc(raw_landed[half % (2 * SLOTS)], 16)

            def load_tall(view, unit_base, n):
                with sp.Fori(0, n // 4) as i:
                    for j in range(8):
                        load(2 * unit_base + j, i, view[:, :, bass.ds((8 * i + j) * P, P)])

            def load_rows(view, unit_base, n):
                with sp.Fori(0, n // 4) as i:
                    for j in range(8):
                        load(2 * unit_base + j, i, view[:, bass.ds(8 * i + j, 1), :])

            def load_tables(ln):
                if ln == 0:
                    sp.wait_ge(ret_decayed, HEADS)
                else:
                    sp.wait_ge(ln_done, EVENTS * ln)
                sp.dma_start(ln_tab[:, 0, :], ln_gain[ln // 2, ln % 2].partition_broadcast(P)) \
                  .then_inc(tab_landed, 16)
                sp.dma_start(ln_tab[:, 1, :], ln_bias[ln // 2, ln % 2].partition_broadcast(P)) \
                  .then_inc(tab2_landed, 16)

            for j in range(2 * N_PROJ):
                if j < PIECES:
                    s = slice(j * PW, (j + 1) * PW)
                    sp.dma_start(resid[:, :, s], x_v[:, :, s]).then_inc(x_landed[j], 16)
                c = GROUP_COLUMN[j // 4]
                load(j, 0, w_in_v[:, 2 * (j % 4):2 * (j % 4) + 2, c:c + RW])
                if j == 15:
                    sp.dma_start(decay_t, decay.rearrange("p (h i) -> p h i", h=HEADS)) \
                      .then_inc(decay_landed, 16)
                    sp.dma_start(gn_gain, ret_gn_gain[0].partition_broadcast(P)) \
                      .then_inc(gain_landed, 16)
            for j in range(2 * N_OUT):
                k = (4 + j) % KD
                load(2 * U_OUT + j, 0, w_out_v[:, k, :])
            load_tables(0)
            sp.wait_ge(gate_ready, NT)
            sp.wait_ge(moba_masked, HEADS)
            sp.dma_start(ws_n, gmlp_w_s[0].rearrange("g i j -> i g j")).then_inc(ws_landed, 16)
            sp.dma_start(rows48[0:GM, :], gmlp_b_uv[0, 0:GW].rearrange("(m c) -> m c", m=GM)) \
              .then_inc(rows_landed[0], 16)
            sp.dma_start(rows48[GM:2 * GM, :], gmlp_ln_gain[0].rearrange("(m c) -> m c", m=GM)) \
              .then_inc(rows_landed[1], 16)
            sp.dma_start(rows48[2 * GM:3 * GM, :], gmlp_ln_bias[0].rearrange("(m c) -> m c", m=GM)) \
              .then_inc(rows_landed[2], 16)
            sp.wait_ge(ret_out, 1)
            sp.dma_start(b_s_all, gmlp_b_s[0].partition_broadcast(P)).then_inc(bs_landed, 16)
            load_tall(w1_v[0], U_FA, N_FF)
            load_tables(1)
            load_rows(w2_v[0], U_FB, N_FF)
            sp.wait_ge(spatial_add_ready, GM)
            sp.dma_start(v_bias, gmlp_b_uv[0, GW:2 * GW].partition_broadcast(P)).then_inc(vb_landed, 16)
            with sp.Fori(0, N_GV // 4) as i:
                for j in range(8):
                    c = GW + (2 * i + j // 4) * RW
                    load(2 * U_GV + j, i, w_uv_v[:, 2 * (j % 4):2 * (j % 4) + 2, bass.ds(c, RW)])
            load_tables(2)
            load_tall(w_uv_v, U_GU, N_GU)
            load_rows(w_go_v, U_GO, N_GO)
            load_tall(w1_v[1], U_FC, N_FF)
            load_tables(3)
            load_rows(w2_v[1], U_FD, N_FF)
            for t in range(NT):
                for n in range(2):
                    sp.wait_ge(ln_done, EVENTS * (LNS - 1) + OUT_ORDER.index((t, 2 * n + 1)) + 1)
                    s = slice(n * HALF_D, (n + 1) * HALF_D)
                    sp.dma_start(out_v[:, t, s], resid[:, t, s]).then_inc(out_written[2 * t + n], 16)
            for s in out_written:
                sp.wait_ge(s, 16)

        @block.gpsimd
        def _(pool):
            step = Count(pool, pool_step)
            nc.gpsimd.memset(ones[:, :], 1.0).then_inc(ones_ready, 1)
            step.inc(nc.gpsimd.memset(ident[:, :], 0.0))
            step.inc(nc.gpsimd.memset(causal, 0.0))
            nc.gpsimd.memset(half_pi, float(np.pi / 2)).then_inc(half_pi_ready, 1)
            step.wait()
            nc.gpsimd.affine_select(out=ident[:, :], in_=ident[:, :], compare_op=ALU.not_equal,
                                    fill=1.0, base=0, pattern=[[-1, P]], channel_multiplier=1) \
                .then_inc(consts_ready, 1)
            lower = causal[:, P:3 * P]
            nc.gpsimd.affine_select(out=lower, in_=lower, compare_op=ALU.is_ge, fill=MASKED, base=0,
                                    pattern=[[0, 2], [-1, P]], channel_multiplier=1) \
                .then_inc(consts_ready, 1)

            def angle_part(n):
                w = NT * ROPE_HALF
                return work[:, 0, n * w:(n + 1) * w].rearrange("p (t f) -> p t f", t=NT)

            def angles():
                pool.wait_ge(rope_in_landed, 16)
                step.inc(nc.gpsimd.tensor_copy(pos_f, pos_i[:, :]))
                pool.wait_ge(freq_landed, 16)
                step.wait()
                for t in range(NT):
                    step.inc(nc.gpsimd.tensor_scalar(ang[:, t, :], freq[:, :], pos_f[:, t:t + 1], None, ALU.mult))
                step.wait()
                magic = 1.5 * 2.0 ** 23
                for level, parts in ((24, 6), (12, 5), (0, 4)):
                    period = 2.0 * np.pi * 2.0 ** level
                    step.inc(nc.gpsimd.tensor_scalar(turns[:, :, :], ang[:, :, :], float(1.0 / period), magic,
                                                     ALU.mult, ALU.add))
                    step.wait()
                    step.inc(nc.gpsimd.tensor_scalar(turns[:, :, :], turns[:, :, :], magic, None, ALU.subtract))
                    step.wait()
                    period_parts = split_bits(period, 11, parts)
                    made = [step.inc(nc.gpsimd.tensor_scalar(angle_part(n), turns[:, :, :], part, None, ALU.mult))
                            for n, part in enumerate(period_parts)]
                    for n in range(len(period_parts)):
                        step.wait(made[n] if n == 0 else None)
                        step.inc(nc.gpsimd.tensor_tensor(ang[:, :, :], ang[:, :, :], angle_part(n), ALU.subtract))
                    step.wait()
                pi_below = 3.1415925
                nc.gpsimd.tensor_scalar(ang[:, :, :], ang[:, :, :], pi_below, -pi_below, ALU.min, ALU.max) \
                    .then_inc(angles_ready, 1)

            angles()

            for r in range(len(ROTATED)):
                for t in range(NT):
                    pool.wait_ge(rope_products, 3 * (NT * r + t) + 3)
                    if r >= 2:
                        pool.wait_ge(qk_turned, NT * (r - 2) + t + 1)
                    nc.gpsimd.tensor_tensor(qk_n[r % 2][:, t, :], work[:, t, 0:RW],
                                            work[:, t, RW:2 * RW], ALU.add).then_inc(rope_added, 1)

            pool.wait_ge(gain_landed, 16)
            for t in range(NT):
                pool.wait_ge(gate_silu, t + 1)
                nc.gpsimd.tensor_tensor(gate[:, t, :], gate[:, t, :], gn_gain, ALU.mult) \
                    .then_inc(gate_ready, 1)

            def squares(tile_base):
                with pool.Fori(0, FM // 8) as i:
                    for j in range(8):
                        pool.wait_ge(act_out, tile_base + 8 * i + j + 1)
                        h = hidden[:, bass.ds(8 * i + j, 1), :]
                        nc.gpsimd.tensor_tensor(h, h, h, ALU.mult).then_inc(hidden_ready, 1)

            pool.wait_ge(ws_landed, 16)
            nc.gpsimd.affine_select(out=ws_n, in_=ws_n, compare_op=ALU.is_ge, fill=0.0, base=0,
                                    pattern=[[0, GROUPS], [-1, P]], channel_multiplier=1) \
                .then_inc(ws_masked, 1)
            squares(0)
            with pool.Fori(0, GM // 8) as i:
                for j in range(8):
                    pool.wait_ge(act_out, FM + 8 * i + j + 1)
                    pool.wait_ge(mixed_ready, 8 * i + j + 1)
                    nc.gpsimd.tensor_tensor(hidden[:, bass.ds(8 * i + j, 1), :],
                                            mixed[:, j % 2:j % 2 + 1, :], u_tile[:, j % 4:j % 4 + 1, :],
                                            ALU.mult).then_inc(hidden_ready, 1)
            squares(FM + GM)

        @block.scalar
        def _(act):
            def ln_scalar(ln, t):
                act.wait_ge(ln_var, NT * ln + t + 1)
                nc.scalar.activation(ln_rstd[:, t:t + 1], ln_rstd[:, t:t + 1], ACT.Sqrt) \
                    .then_inc(ln_std, 1)

            def xt_piece(turned, e, order):
                t, q = order[e]
                act.wait_ge(xt_turned, turned + e + 1)
                nc.scalar.activation(xt_high[:, 2 * q:2 * q + 2, t * P:(t + 1) * P], piece_tiles(order, e),
                                     ACT.Copy).then_inc(xt_high_ready, 1)

            def qk_out(g):
                for t in range(NT):
                    act.wait_ge(qk_turned, NT * ROTATED.index(g) + t + 1)
                    nc.scalar.activation(qk_t[g][:, :, t * P:(t + 1) * P],
                                         ps_m[:, 2 * (g % 2) + t, :].rearrange("p (k c) -> p k c", k=4),
                                         ACT.Copy).then_inc(qk_t_ready, 1)

            def v_out(g):
                act.wait_ge(w_used, 4 * (g + 1))
                for t in range(NT):
                    nc.scalar.activation(v_n[g][:, t, :], ps_m[:, 2 * (g % 2) + t, :],
                                         ACT.Copy).then_inc(v_ready, 1)

            def exps(batch):
                act.wait_ge(moba_max, batch + 1)
                for h in range(4 * batch, 4 * batch + 4):
                    for t, s in ((1, slice(0, 2 * P)), (0, slice(2 * P, 3 * P))):
                        c = t * HEADS + h
                        nc.scalar.activation(p_moba[:, h, s], p_moba[:, h, s], ACT.Exp,
                                             bias=neg_mx[:, c:c + 1], scale=QK_SCALE,
                                             accum_out=p_sum[:, c:c + 1]).then_inc(moba_exp, 1)

            def p_out(h):
                act.wait_ge(p_turned, h + 1)
                nc.scalar.activation(p_moba[:, h, :], ps_y[:, h % 4, 0:3 * P], ACT.Copy) \
                    .then_inc(p_t_ready, 1)

            act.dma_start(pos_i[:, :], positions.rearrange("a (t p) -> p (a t)", p=P),
                           allow_slow_non_contiguous=True) \
                .then_inc(rope_in_landed, 16)
            act.dma_start(freq[:, :], inv_freq.partition_broadcast(P)).then_inc(freq_landed, 16)
            for j, q in ((0, 0), (1, 1), (2, None), (3, 2), (4, 3), (5, None)):
                if q is not None:
                    for t in range(NT):
                        xt_piece(0, NT * q + t, IN_ORDER)
                split_high(act, 0, j)

            for j in range(2 * N_PROJ):
                ahead(split_high, act, 0, j)
                if j == 1:
                    act.wait_ge(angles_ready, 1)
                    act.wait_ge(half_pi_ready, 1)
                    nc.scalar.activation(turns[:, :, :], ang[:, :, :], ACT.Abs).then_inc(abs_ready, 1)
                    nc.scalar.activation(sin2[:, :, 0:ROPE_HALF], ang[:, :, :], ACT.Sin, scale=-1.0) \
                        .then_inc(rope_tab_ready, 1)
                    nc.scalar.activation(sin2[:, :, ROPE_HALF:HD], ang[:, :, :], ACT.Sin) \
                        .then_inc(rope_tab_ready, 1)
                    act.wait_ge(abs_ready, 1)
                    for s in (slice(0, ROPE_HALF), slice(ROPE_HALF, HD)):
                        nc.scalar.activation(cos2[:, :, s], turns[:, :, :], ACT.Sin, bias=half_pi,
                                             scale=-1.0).then_inc(rope_tab_ready, 1)
                if j in (6, 10, 18, 22):
                    qk_out((QB, KB, None, QA, KA)[(j - 6) // 4])
                if j == 12:
                    v_out(VB)
                if j == 13:
                    exps(0)
                if j == 15:
                    exps(1)
                if 16 <= j < 20:
                    for h in (2 * (j - 16), 2 * (j - 16) + 1):
                        p_out(h)
                if j == 22:
                    for t in range(NT):
                        act.wait_ge(c_turned, t + 1)
                        nc.scalar.activation(ht_high[:, :, t * P:(t + 1) * P],
                                             ps_y[:, t, :].rearrange("p (k c) -> p k c", k=4), ACT.Copy) \
                            .then_inc(c_high_ready, 1)
                if j == 24:
                    v_out(VA)
            act.wait_ge(gn_var, 1)
            nc.scalar.activation(gn_rstd, gn_rstd, ACT.Sqrt).then_inc(gn_std, 1)
            act.wait_ge(w_used, 4 * (GA + 1))
            for t in range(NT):
                nc.scalar.activation(gate[:, t, :], ps_m[:, 2 * (GA % 2) + t, :], ACT.Silu) \
                    .then_inc(gate_silu, 1)
            for j in range(2):
                ahead(split_high, act, U_OUT, j)
            for t in range(NT):
                act.wait_ge(c_turned, NT + t + 1)
                nc.scalar.activation(xt_high[:, 0:4, t * P:(t + 1) * P],
                                     ps_m[:, 2 + t, :].rearrange("p (k c) -> p k c", k=4), ACT.Copy) \
                    .then_inc(c_high_ready, 1)
            for j in range(2, 4):
                ahead(split_high, act, U_OUT, j)

            def tail(ln, unit_base):
                for j in range(SPLIT_FIRST[ln]):
                    ahead(split_high, act, unit_base, j)
                ln_scalar(ln, 0)
                if ln == LNS - 1:
                    ln_scalar(ln, 1)
                    return
                for e in range(EVENTS):
                    if LN_ORDERS[ln][e] == (1, 0):
                        ln_scalar(ln, 1)
                    xt_piece(EVENTS * (ln + 1), e, LN_ORDERS[ln])
                for j in range(SPLIT_FIRST[ln], 4):
                    ahead(split_high, act, unit_base, j)

            tail(0, U_OUT + 2)

            def tall_stage(unit_base, n, tile_base, finish, ready, after_first=None):
                def tile(i, j):
                    ahead(split_high, act, unit_base, j, i)
                    if isinstance(i, int) and 8 * i + j == 2 * n - 1:
                        for k in range(2):
                            hidden_high(k, ready, 2 * (unit_base + n))
                    act.wait_ge(w_used, 2 * unit_base + 8 * i + j + 1)
                    finish(i, j, ps_m[:, j % 4, 0:SEQ]).then_inc(act_out, 1)

                bodies = n // 4
                first = 0
                if after_first is not None:
                    for j in range(8):
                        tile(0, j)
                    after_first()
                    first = 1
                with act.Fori(first, bodies - 1) as i:
                    for j in range(8):
                        tile(i, j)
                for j in range(8):
                    tile(bodies - 1, j)

            def relu_tile(i, j, bank):
                return nc.scalar.activation(hidden[:, bass.ds(8 * i + j, 1), :].rearrange("p a b -> p (a b)"),
                                            bank, ACT.Relu)

            def hidden_high(n, ready, half, i=0):
                act.wait_ge(hidden_ready, ready + n + 1 + 8 * i)
                act.wait_ge(w_used, half + n - 4 + 1 + 8 * i)
                src = hidden[:, n, :] if isinstance(i, int) and i == 0 else \
                    hidden[:, bass.ds(8 * i + n, 1), :].rearrange("p a b -> p (a b)")
                nc.scalar.activation(ht_high[:, n % 4, :], src, ACT.Copy).then_inc(ht_high_ready, 1)

            def rows_stage(ln, unit_base, tiles, ready):
                loops = (tiles - 4) // 8
                if loops > 1:
                    with act.Fori(0, loops) as i:
                        for j in range(8):
                            ahead(split_high, act, unit_base, j, i)
                            hidden_high(j + 2, ready, 2 * unit_base, i)
                for n in range(8 * loops if loops > 1 else 0, tiles - 4):
                    ahead(split_high, act, unit_base, n)
                    hidden_high(n + 2, ready, 2 * unit_base)
                for n in range(tiles - 2, tiles):
                    hidden_high(n, ready, 2 * unit_base)
                tail(ln, unit_base + tiles // 2 - 2)

            def small_tables():
                act.wait_ge(ws_turned, 3)
                nc.scalar.activation(cols48[:, :], ps_y[:, 2, 0:3 * GM], ACT.Copy).then_inc(ws_t_ready, 1)
                for b in range(2):
                    nc.scalar.activation(ws_t[:, 4 * b:4 * b + 4, :],
                                         ps_y[:, b, :].rearrange("p (g c) -> p g c", g=4),
                                         ACT.Copy).then_inc(ws_t_ready, 1)

            tall_stage(U_FA, N_FF, 0, relu_tile, 0, small_tables)
            rows_stage(1, U_FB, FM, 0)

            with act.Fori(0, N_GV // 4) as i:
                for j in range(8):
                    ahead(split_high, act, U_GV, j, i)
                    if j % 4 == 3:
                        for t in range(NT):
                            act.wait_ge(v_biased, 4 * i + 2 * (j // 4) + t + 1)
                            v = v_gate[:, t, bass.ds((2 * i + j // 4) * RW, RW)]
                            nc.scalar.activation(v, v, ACT.Gelu_apprx_tanh).then_inc(v_gelu, 1)
            act.wait_ge(v_var, 1)
            nc.scalar.activation(v_rstd, v_rstd, ACT.Sqrt).then_inc(v_std, 1)
            for j in range(2 * N_GU):
                ahead(split_high, act, U_GU, j)
                if j == 2 * N_GU - 1:
                    for k in range(2):
                        hidden_high(k, FM, 2 * U_GO)
                act.wait_ge(w_used, 2 * U_GU + j + 1)
                if j >= 4:
                    act.wait_ge(hidden_ready, FM + j - 3)
                nc.scalar.activation(u_tile[:, j % 4, :], ps_m[:, j % 4, 0:SEQ], ACT.Gelu_apprx_tanh,
                                     bias=cols48[:, j:j + 1]).then_inc(act_out, 1)
            rows_stage(2, U_GO, GM, FM)
            tall_stage(U_FC, N_FF, FM + GM, relu_tile, FM + GM)
            rows_stage(3, U_FD, FM, FM + GM)

        @block.vector
        def _(dve):
            step = Count(dve, dve_step)
            def xt_piece(turned, e, order):
                t, q = order[e]
                dve.wait_ge(xt_high_ready, turned + e + 1)
                s = (slice(None), slice(2 * q, 2 * q + 2), slice(t * P, (t + 1) * P))
                nc.vector.tensor_tensor(xt_low[s], piece_tiles(order, e), xt_high[s], ALU.subtract) \
                    .then_inc(xt_low_ready, 1)

            def rstd_of(var, out_cols):
                step.inc(nc.vector.tensor_scalar(out_cols, var, EPS, None, ALU.add))
                step.wait()
                return nc.vector.reciprocal(out_cols, out_cols)

            def add_resid(ln, block, end):
                if block == LAST_BLOCK:
                    dve.wait_ge(w_used, end)
                else:
                    dve.wait_ge(y_done, LAST_BLOCK * ln + block + 1)
                t, start, width = Y_BLOCKS[block]
                s = slice(start, start + width)
                step.inc(nc.vector.scalar_tensor_tensor(
                    out=work[:, t, s], in0=resid[:, t, s], scalar=ALPHA, in1=y_bank(block),
                    op0=ALU.mult, op1=ALU.add))
                step.wait()
                for q in range(start // PW, (start + width) // PW):
                    c = 6 * (4 * t + q)
                    step.inc(nc.vector.bn_stats(ln_stats[:, c:c + 6], work[:, t, q * PW:(q + 1) * PW]))

            def variance(ln, t):
                step.wait()
                mv = ln_mv[:, 2 * t:2 * t + 2]
                step.inc(nc.vector.bn_aggr(mv, ln_stats[:, 24 * t:24 * t + 24]))
                step.wait()
                rstd_of(mv[:, 1:2], ln_rstd[:, t:t + 1]).then_inc(ln_var, 1)

            def centre(e, order):
                t, q = order[e]
                s = slice(q * PW, (q + 1) * PW)
                return step.inc(nc.vector.scalar_tensor_tensor(
                    out=work[:, t, s], in0=work[:, t, s], scalar=ln_mv[:, 2 * t:2 * t + 1],
                    in1=ln_tab[:, 0, s], op0=ALU.subtract, op1=ALU.mult))

            def scale(ln, e, order, centred):
                t, q = order[e]
                s = slice(q * PW, (q + 1) * PW)
                dve.wait_ge(ln_std, NT * ln + t + 1)
                step.wait(centred)
                nc.vector.scalar_tensor_tensor(out=resid[:, t, s], in0=work[:, t, s],
                                               scalar=ln_rstd[:, t:t + 1], in1=ln_tab[:, 1, s],
                                               op0=ALU.mult, op1=ALU.add).then_inc(ln_done, 1)

            def layer_norm(ln, end):
                order = LN_ORDERS[ln]
                first = order.index((1, 0))
                lows = [0]

                def low_parts(upto):
                    while lows[0] <= upto and ln < LNS - 1:
                        xt_piece(EVENTS * (ln + 1), lows[0], order)
                        lows[0] += 1

                for block in (0, 1):
                    add_resid(ln, block, end)
                variance(ln, 0)
                dve.wait_ge(tab_landed, 16 * (ln + 1))
                dve.wait_ge(tab2_landed, 16 * (ln + 1))
                centred = [centre(0, order)]
                for e in range(first):
                    if e + 1 < first:
                        centred.append(centre(e + 1, order))
                    scale(ln, e, order, centred[e])
                if order is OUT_ORDER:
                    low_parts(1)
                add_resid(ln, 2, end)
                if order is OUT_ORDER:
                    low_parts(3)
                add_resid(ln, 3, end)
                add_resid(ln, 4, end)
                variance(ln, 1)
                centred.append(centre(first, order))
                low_parts(0)
                scale(ln, first, order, centred[first])
                centred.append(centre(first + 1, order))
                for e in range(first + 1, EVENTS):
                    low_parts(e - 2)
                    if e + 1 < EVENTS and ln == LNS - 1:
                        centred.append(centre(e + 1, order))
                    scale(ln, e, order, centred[e])
                    if e + 1 < EVENTS and ln < LNS - 1:
                        centred.append(centre(e + 1, order))
                low_parts(EVENTS - 1)

            for j, q in ((0, 0), (1, 1), (2, None), (3, 2), (4, 3), (5, None)):
                if q is not None:
                    for t in range(NT):
                        xt_piece(0, NT * q + t, IN_ORDER)
                split_low(dve, 0, j)

            def rope(g):
                dve.wait_ge(w_used, 4 * (g + 1))
                r = ROTATED.index(g)
                if r == 0:
                    dve.wait_ge(rope_tab_ready, 4)
                for t in range(NT):
                    if r > 0:
                        dve.wait_ge(rope_added, NT * (r - 1) + t + 1)
                    src = ps_m[:, 2 * (g % 2) + t, :].rearrange("p (h d) -> p h d", h=HEADS)
                    a = work[:, t, 0:RW].rearrange("p (h d) -> p h d", h=HEADS)
                    b = work[:, t, RW:2 * RW].rearrange("p (h d) -> p h d", h=HEADS)
                    wide_cos = cos2[:, t:t + 1, :].to_broadcast([P, HEADS, HD])
                    wide_sin = sin2[:, t:t + 1, :].to_broadcast([P, HEADS, HD])
                    nc.vector.tensor_tensor(a, src, wide_cos, ALU.mult).then_inc(rope_products, 1)
                    for to, of in ((slice(0, ROPE_HALF), slice(ROPE_HALF, HD)),
                                   (slice(ROPE_HALF, HD), slice(0, ROPE_HALF))):
                        nc.vector.tensor_tensor(b[:, :, to], src[:, :, of], wide_sin[:, :, to],
                                                ALU.mult).then_inc(rope_products, 1)

            def moba_mask(batch):
                if batch == 0:
                    dve.wait_ge(consts_ready, 2)
                for h in range(4 * batch, 4 * batch + 4):
                    dve.wait_ge(moba_scores, h + 1)
                    nc.vector.tensor_tensor(p_moba[:, h, :], ps_y[:, h % 4, 0:3 * P], causal,
                                            ALU.add).then_inc(moba_masked, 1)
                hs = slice(4 * batch, 4 * batch + 4)
                dve.wait_ge(moba_masked, 4 * batch + 4)
                for t, s in ((1, slice(0, 2 * P)), (0, slice(2 * P, 3 * P))):
                    step.inc(nc.vector.tensor_reduce(mx[:, t * HEADS:(t + 1) * HEADS][:, hs], p_moba[:, hs, s],
                                                     AX_X, ALU.max))
                step.wait()
                two = lambda c: c.rearrange("p (t h) -> p t h", t=2)[:, :, hs]
                nc.vector.tensor_scalar(two(neg_mx), two(mx), -QK_SCALE, None, ALU.mult).then_inc(moba_max, 1)

            def ret_decay(batch):
                if batch == 0:
                    dve.wait_ge(decay_landed, 16)
                for h in range(4 * batch, 4 * batch + 4):
                    dve.wait_ge(ret_scores, h + 1)
                    nc.vector.tensor_tensor(p_ret[:, h, 0:2 * P], ps_y[:, h % 4, 0:2 * P],
                                            decay_t[:, h, :], ALU.mult)
                    nc.vector.tensor_tensor(p_ret[:, h, 2 * P:3 * P], ps_y[:, h % 4, 2 * P:3 * P],
                                            decay_t[:, h, 0:P], ALU.mult).then_inc(ret_decayed, 1)

            def per_head(c):
                return c.unsqueeze(2).to_broadcast([P, HEADS, HD])

            def moba_output():
                dve.wait_ge(moba_exp, 2 * HEADS)
                step.inc(nc.vector.reciprocal(p_inv, p_sum))
                step.wait()
                dve.wait_ge(moba_out, 1)
                for t in range(NT):
                    nc.vector.tensor_tensor(y_moba[:, t, :].rearrange("p (h d) -> p h d", h=HEADS),
                                            ps_y[:, 2 + t, :].rearrange("p (h d) -> p h d", h=HEADS),
                                            per_head(p_inv[:, t * HEADS:(t + 1) * HEADS]),
                                            ALU.mult).then_inc(y_moba_ready, 1)

            gn_pairs = gn_mv.rearrange("p (c two) -> p c two", two=2)

            def group_statistics():
                dve.wait_ge(ret_out, 1)
                for t in range(NT):
                    for h in range(HEADS):
                        c = 6 * (t * HEADS + h)
                        step.inc(nc.vector.bn_stats(gn_stats[:, c:c + 6], ps_m[:, 2 + t, h * HD:(h + 1) * HD]))
                step.wait()
                for c in range(2 * HEADS):
                    step.inc(nc.vector.bn_aggr(gn_mv[:, 2 * c:2 * c + 2], gn_stats[:, 6 * c:6 * c + 6]))
                step.wait()
                rstd_of(gn_pairs[:, :, 1], gn_rstd).then_inc(gn_var, 1)

            def group_norm():
                for t in range(NT):
                    y = y_ret[:, t, :].rearrange("p (h d) -> p h d", h=HEADS)
                    s = slice(t * HEADS, (t + 1) * HEADS)
                    step.inc(nc.vector.tensor_tensor(y, ps_m[:, 2 + t, :].rearrange("p (h d) -> p h d", h=HEADS),
                                                     per_head(gn_pairs[:, s, 0]), ALU.subtract))
                dve.wait_ge(gn_std, 1)
                step.wait()
                for t in range(NT):
                    y = y_ret[:, t, :].rearrange("p (h d) -> p h d", h=HEADS)
                    step.inc(nc.vector.tensor_tensor(y, y, per_head(gn_rstd[:, t * HEADS:(t + 1) * HEADS]),
                                                     ALU.mult))
                step.wait()

            rope_at = {2: QB, 8: KB, 16: QA, 20: KA}
            for j in range(2 * N_PROJ):
                if j in rope_at:
                    rope(rope_at[j])
                ahead(split_low, dve, 0, j)
                if j == 12:
                    moba_mask(0)
                if j == 14:
                    moba_mask(1)
                if j == 20:
                    moba_output()
                if j == 22:
                    for t in range(NT):
                        dve.wait_ge(c_high_ready, t + 1)
                        nc.vector.tensor_tensor(ht_low[:, :, t * P:(t + 1) * P],
                                                ps_y[:, t, :].rearrange("p (k c) -> p k c", k=4),
                                                ht_high[:, :, t * P:(t + 1) * P], ALU.subtract) \
                            .then_inc(c_low_ready, 1)
                if j == 24:
                    ret_decay(0)
                if j == 25:
                    ret_decay(1)
                if j == 26:
                    group_statistics()
            group_norm()
            for t in range(NT):
                dve.wait_ge(gate_ready, t + 1)
                nc.vector.tensor_tensor(y_ret[:, t, :], y_ret[:, t, :], gate[:, t, :],
                                        ALU.mult).then_inc(y_ret_ready, 1)
            for j in range(2):
                ahead(split_low, dve, U_OUT, j)
            for t in range(NT):
                dve.wait_ge(c_high_ready, NT + t + 1)
                nc.vector.tensor_tensor(xt_low[:, 0:4, t * P:(t + 1) * P],
                                        ps_m[:, 2 + t, :].rearrange("p (k c) -> p k c", k=4),
                                        xt_high[:, 0:4, t * P:(t + 1) * P], ALU.subtract) \
                    .then_inc(c_low_ready, 1)
            for j in range(2, 4):
                ahead(split_low, dve, U_OUT, j)

            def tail(ln, unit_base):
                for j in range(SPLIT_FIRST[ln]):
                    ahead(split_low, dve, unit_base, j)
                layer_norm(ln, 2 * unit_base + 4)
                for j in range(SPLIT_FIRST[ln], 4):
                    ahead(split_low, dve, unit_base, j)

            tail(0, U_OUT + 2)

            def tall_stage(unit_base, n):
                with dve.Fori(0, n // 4) as i:
                    for j in range(8):
                        ahead(split_low, dve, unit_base, j, i)

            def hidden_low(n, seen, i=0):
                dve.wait_ge(ht_high_ready, seen + n + 1 + 8 * i)
                src = hidden[:, n, :] if isinstance(i, int) and i == 0 else \
                    hidden[:, bass.ds(8 * i + n, 1), :].rearrange("p a b -> p (a b)")
                nc.vector.tensor_tensor(ht_low[:, n % 4, :], src, ht_high[:, n % 4, :], ALU.subtract) \
                    .then_inc(ht_low_ready, 1)

            def rows_stage(ln, unit_base, tiles, seen, between=None):
                for n in range(2):
                    hidden_low(n, seen)
                loops = (tiles - 4) // 8
                if loops > 1:
                    with dve.Fori(0, loops) as i:
                        for j in range(8):
                            ahead(split_low, dve, unit_base, j, i)
                            hidden_low(j + 2, seen, i)
                if between is not None:
                    between()
                for n in range(8 * loops if loops > 1 else 0, tiles - 4):
                    ahead(split_low, dve, unit_base, n)
                    hidden_low(n + 2, seen)
                for n in range(tiles - 2, tiles):
                    hidden_low(n, seen)
                tail(ln, unit_base + tiles // 2 - 2)

            def spatial_table():
                dve.wait_ge(row_sums, 2)
                dve.wait_ge(bs_landed, 16)
                dve.wait_ge(ws_t_ready, 3)
                for m in range(GM):
                    g = m // 2
                    bank = 3 if g < 4 else 0
                    nc.vector.scalar_tensor_tensor(out=spatial_add[:, m, :],
                                                   in0=ps_m[:, bank, (g % 4) * P:(g % 4 + 1) * P],
                                                   scalar=cols48[:, 2 * GM + m:2 * GM + m + 1],
                                                   in1=b_s_all[:, g, :], op0=ALU.mult, op1=ALU.add) \
                        .then_inc(spatial_add_ready, 1)

            tall_stage(U_FA, N_FF)
            rows_stage(1, U_FB, FM, 0, spatial_table)

            dve.wait_ge(vb_landed, 16)
            with dve.Fori(0, N_GV // 4) as i:
                for j in range(8):
                    ahead(split_low, dve, U_GV, j, i)
                    if j % 4 == 3:
                        g = j // 4
                        dve.wait_ge(w_used, 2 * U_GV + 8 * i + j + 1)
                        for t in range(NT):
                            nc.vector.tensor_tensor(v_gate[:, t, bass.ds((2 * i + g) * RW, RW)],
                                                    ps_m[:, 2 * g + t, :], v_bias[:, bass.ds((2 * i + g) * RW, RW)],
                                                    ALU.add).then_inc(v_biased, 1)
                        for t in range(NT):
                            dve.wait_ge(v_gelu, 4 * i + 2 * g + t + 1)
                            nc.vector.bn_stats(v_stats[:, bass.ds(24 * t + 6 * (2 * i + g), 6)],
                                               v_gate[:, t, bass.ds((2 * i + g) * RW, RW)]).then_inc(v_stat, 1)
            dve.wait_ge(v_stat, 4 * NT)
            for t in range(NT):
                step.inc(nc.vector.bn_aggr(v_mv[:, 2 * t:2 * t + 2], v_stats[:, 24 * t:24 * t + 24]))
            step.wait()
            rstd_of(v_mv.rearrange("p (t two) -> p t two", two=2)[:, :, 1], v_rstd).then_inc(v_var, 1)
            dve.wait_ge(v_std, 1)

            def normalise(m):
                for t in range(NT):
                    nc.vector.tensor_scalar(vn_tile[:, m % 2, t, :], v_gate[:, t, m * P:(m + 1) * P],
                                            v_mv[:, 2 * t:2 * t + 1], v_rstd[:, t:t + 1],
                                            ALU.subtract, ALU.mult).then_inc(vn_ready, 1)

            def mix(m):
                dve.wait_ge(hidden_ready, FM - 1 + m)
                nc.vector.scalar_tensor_tensor(
                    out=mixed[:, m % 2, :].rearrange("p (t c) -> p t c", t=NT),
                    in0=ps_y[:, m % 4, 0:SEQ].rearrange("p (t c) -> p t c", t=NT),
                    scalar=cols48[:, GM + m:GM + m + 1],
                    in1=spatial_add[:, m:m + 1, :].to_broadcast([P, NT, P]),
                    op0=ALU.mult, op1=ALU.add).then_inc(mixed_ready, 1)

            dve.wait_ge(spatial_add_ready, GM)
            normalise(0)
            normalise(1)
            for m in range(GM):
                ahead(split_low, dve, U_GU, m)
                dve.wait_ge(spatial_done, m + 1)
                if m + 2 < GM:
                    normalise(m + 2)
                mix(m)
            rows_stage(2, U_GO, GM, FM)
            tall_stage(U_FC, N_FF)
            rows_stage(3, U_FD, FM, FM + GM)

        @block.tensor
        def _(pe):
            def turn(bank, src, n=4):
                for c in range(n):
                    last = nc.tensor.transpose(bank[:, c * P:(c + 1) * P], src[:, c * P:(c + 1) * P], ident[:, :])
                return last

            def turn_piece(turned, e, order):
                t, q = order[e]
                if e >= TURNS:
                    pe.wait_ge(xt_low_ready, turned + e - TURNS + 1)
                turn(piece_bank(order, e), resid[:, t, q * PW:(q + 1) * PW], 2) \
                    .then_inc(xt_turned, 1)

            def turn_ln(ln, e):
                pe.wait_ge(ln_done, EVENTS * ln + e + 1)
                turn_piece(EVENTS * (ln + 1), e, LN_ORDERS[ln])

            def wide_products(slot, quarter, t, bank):
                hi, lo = wide(w_high, slot), wide(w_low, slot)
                s = slice(t * P, (t + 1) * P)
                for k in (2 * quarter, 2 * quarter + 1):
                    k4 = k % 4
                    nc.tensor.matmul(bank, xt_high[:, k, s], hi[:, k4, :], start=(k == 0), stop=False)
                    nc.tensor.matmul(bank, xt_high[:, k, s], lo[:, k4, :], start=False, stop=False)
                    mm = nc.tensor.matmul(bank, xt_low[:, k, s], hi[:, k4, :], start=False,
                                          stop=(k == KD - 1))
                return mm

            def wide_half(slot, quarter, banks):
                for t in range(NT):
                    mm = wide_products(slot, quarter, t, banks[t])
                return mm

            def warm(n):
                for _ in range(n):
                    nc.tensor.matmul(ps_m[:, 0, 0:P], ones[:, :], ones[:, :], start=True, stop=True)

            def turn_input(q):
                pe.wait_ge(x_landed[q], 16)
                for t in range(NT):
                    turn_piece(0, NT * q + t, IN_ORDER)

            pe.wait_ge(ones_ready, 1)
            warm(6)
            pe.wait_ge(consts_ready, 1)
            turn_input(0)
            warm(2)
            turn_input(1)
            warm(2)

            def turn_qk(g):
                r = ROTATED.index(g)
                for t in range(NT):
                    pe.wait_ge(rope_added, NT * r + t + 1)
                    turn(ps_m[:, 2 * (g % 2) + t, :], qk_n[r % 2][:, t, :]).then_inc(qk_turned, 1)

            def scores_moba(pair):
                for h in (2 * pair, 2 * pair + 1):
                    rows = slice((h % 2) * HD, (h % 2 + 1) * HD)
                    if h >= 4:
                        pe.wait_ge(moba_masked, h - 3)
                    q, k = qk_t[QB][rows, pair, :], qk_t[KB][rows, pair, :]
                    bank = ps_y[:, h % 4, :]
                    nc.tensor.matmul(bank[:, 0:2 * P], q[:, P:2 * P], k[:, 0:2 * P], start=True, stop=True)
                    nc.tensor.matmul(bank[:, 2 * P:3 * P], q[:, 0:P], k[:, 0:P], start=True, stop=True) \
                        .then_inc(moba_scores, 1)

            def scores_ret(pair):
                for h in (2 * pair, 2 * pair + 1):
                    rows = slice((h % 2) * HD, (h % 2 + 1) * HD)
                    if h >= 4:
                        pe.wait_ge(ret_decayed, h - 3)
                    q, k = qk_t[QA][rows, pair, :], qk_t[KA][rows, pair, :]
                    bank = ps_y[:, h % 4, :]
                    nc.tensor.matmul(bank[:, 0:2 * P], k[:, 0:P], q[:, 0:2 * P], start=True, stop=True)
                    nc.tensor.matmul(bank[:, 2 * P:3 * P], k[:, P:2 * P], q[:, P:2 * P], start=True, stop=True) \
                        .then_inc(ret_scores, 1)

            def turn_p(h):
                pe.wait_ge(moba_exp, 2 * h + 2)
                if h < 4:
                    pe.wait_ge(moba_masked, h + 5)
                else:
                    pe.wait_ge(p_t_ready, h - 3)
                turn(ps_y[:, h % 4, :], p_moba[:, h, :], 3).then_inc(p_turned, 1)

            def values_moba():
                pe.wait_ge(v_ready, NT)
                pe.wait_ge(p_t_ready, HEADS)
                for h in range(HEADS):
                    c = slice(h * HD, (h + 1) * HD)
                    w = p_moba[:, h, :]
                    nc.tensor.matmul(ps_y[:, 3, c], w[:, 0:P], v_n[VB][:, 0, c], start=True, stop=False)
                    nc.tensor.matmul(ps_y[:, 3, c], w[:, P:2 * P], v_n[VB][:, 1, c], start=False, stop=True)
                    mm = nc.tensor.matmul(ps_y[:, 2, c], w[:, 2 * P:3 * P], v_n[VB][:, 0, c],
                                          start=True, stop=True)
                mm.then_inc(moba_out, 1)

            def values_ret():
                pe.wait_ge(v_ready, 2 * NT)
                for h in range(HEADS):
                    pe.wait_ge(ret_decayed, h + 1)
                    c = slice(h * HD, (h + 1) * HD)
                    w = p_ret[:, h, :]
                    nc.tensor.matmul(ps_m[:, 2, c], w[:, 0:P], v_n[VA][:, 0, c], start=True, stop=True)
                    nc.tensor.matmul(ps_m[:, 3, c], w[:, P:2 * P], v_n[VA][:, 0, c], start=True, stop=False)
                    mm = nc.tensor.matmul(ps_m[:, 3, c], w[:, 2 * P:3 * P], v_n[VA][:, 1, c],
                                          start=False, stop=True)
                mm.then_inc(ret_out, 1)

            def turn_moba_output():
                for t in range(NT):
                    pe.wait_ge(y_moba_ready, t + 1)
                    turn(ps_y[:, t, :], y_moba[:, t, :]).then_inc(c_turned, 1)

            pair_read = {VB: (qk_t_ready, NT), QA: (qk_t_ready, 2 * NT), KA: (v_ready, NT),
                         VA: (qk_t_ready, 3 * NT), GA: (qk_t_ready, 4 * NT)}
            for j in range(2 * N_PROJ):
                g, q = j // 4, j % 4
                if q == 0 and g in pair_read:
                    pe.wait_ge(*pair_read[g])
                if g == 0:
                    if q in (1, 2):
                        turn_input(q + 1)
                    pe.wait_ge(xt_low_ready, pieces_in(IN_ORDER, q))
                pe.wait_ge(w_low_ready, j + 1)
                wide_half((j // 2) % SLOTS, q, [ps_m[:, 2 * (g % 2) + t, :] for t in range(NT)]) \
                    .then_inc(w_used, 1)
                if j in (5, 9, 17, 21):
                    turn_qk((QB, KB, None, QA, KA)[(j - 5) // 4])
                if j == 11:
                    pe.wait_ge(qk_t_ready, 2 * NT)
                    scores_moba(0)
                    scores_moba(1)
                if j == 13:
                    scores_moba(2)
                    scores_moba(3)
                if 15 <= j < 19:
                    turn_p(2 * (j - 15))
                    turn_p(2 * (j - 15) + 1)
                if j == 19:
                    values_moba()
                if j == 21:
                    turn_moba_output()
                if j == 23:
                    pe.wait_ge(qk_t_ready, 4 * NT)
                    pe.wait_ge(c_low_ready, NT)
                    scores_ret(0)
                    scores_ret(1)
                if j == 24:
                    scores_ret(2)
                    scores_ret(3)
                if j == 25:
                    values_ret()

            def rows_products(stationary, block, slot, half, start, stop):
                (hi, lo) = stationary
                t, first_col, width = Y_BLOCKS[block]
                s = slice(t * P, (t + 1) * P)
                c = slice(first_col, first_col + width)
                bank = y_bank(block)
                wh, wl = flat(w_high, slot, half)[:, c], flat(w_low, slot, half)[:, c]
                nc.tensor.matmul(bank, hi[:, s], wh, start=start, stop=False)
                nc.tensor.matmul(bank, hi[:, s], wl, start=False, stop=False)
                return nc.tensor.matmul(bank, lo[:, s], wh, start=False, stop=stop)

            def rows_half(unit_base, j, stationary, start, last_bank_free=None):
                for block in range(len(Y_BLOCKS)):
                    if block == LAST_BLOCK and last_bank_free is not None:
                        pe.wait_ge(*last_bank_free)
                    mm = rows_products(stationary, block, (unit_base + j // 2) % SLOTS, j % 2, start, False)
                mm.then_inc(w_used, 1)

            def rows_tail(ln, unit_base, stationary, ready):
                for block in range(len(Y_BLOCKS)):
                    for j in range(4):
                        if block == 0:
                            pe.wait_ge(w_low_ready, 2 * unit_base + j + 1)
                            ready(j)
                        mm = rows_products(stationary(j), block, (unit_base + j // 2) % SLOTS, j % 2,
                                           False, j == 3)
                        if block == LAST_BLOCK:
                            mm.then_inc(w_used, 1)
                    if block < LAST_BLOCK:
                        mm.then_inc(y_done, 1)
                    if block == LAST_BLOCK - 1 and ln < LNS - 1:
                        turn_ln(ln, 0)
                        turn_ln(ln, 1)

            pe.wait_ge(ret_decayed, HEADS)
            for j in range(4):
                pe.wait_ge(w_low_ready, 2 * U_OUT + j + 1)
                rows_half(U_OUT, j, (ht_high[:, j, :], ht_low[:, j, :]), j == 0,
                          (gate_silu, NT) if j == 0 else None)
                if j == 1:
                    for t in range(NT):
                        pe.wait_ge(y_ret_ready, t + 1)
                        turn(ps_m[:, 2 + t, :], y_ret[:, t, :]).then_inc(c_turned, 1)
            pe.wait_ge(c_low_ready, 2 * NT)
            rows_tail(0, U_OUT + 2, lambda j: (xt_high[:, j, :], xt_low[:, j, :]), lambda j: None)

            def tall_products(slot, half, bank, ks=range(KD)):
                hi, lo = tall(w_high, slot, half), tall(w_low, slot, half)
                for k in ks:
                    nc.tensor.matmul(bank, hi[:, k, :], xt_high[:, k, :], start=(k == 0), stop=False)
                    nc.tensor.matmul(bank, hi[:, k, :], xt_low[:, k, :], start=False, stop=False)
                    mm = nc.tensor.matmul(bank, lo[:, k, :], xt_high[:, k, :], start=False, stop=(k == KD - 1))
                return mm

            def tall_stage(unit_base, n, tile_base, ln, after_first=None):
                def tile(i, j):
                    pe.wait_ge(w_low_ready, 2 * unit_base + 8 * i + j + 1)
                    if not (isinstance(i, int) and tile_base + 8 * i + j < 4):
                        pe.wait_ge(act_out, tile_base + 8 * i + j - 3)
                    tall_products((unit_base + j // 2) % SLOTS, j % 2, ps_m[:, j % 4, 0:SEQ]) \
                        .then_inc(w_used, 1)

                turn_between = {(0, 1): 4, (0, 2): 5, (1, 1): 6, (2, 0): 7}
                for e in (2, 3):
                    turn_ln(ln, e)
                pe.wait_ge(w_low_ready, 2 * unit_base + 3)
                for q in range(PIECES):
                    pe.wait_ge(xt_low_ready, EVENTS * (ln + 1) + pieces_in(LN_ORDER, q))
                    for j in range(3):
                        mm = tall_products((unit_base + j // 2) % SLOTS, j % 2, ps_m[:, j, 0:SEQ],
                                           (2 * q, 2 * q + 1))
                        if q == PIECES - 1:
                            mm.then_inc(w_used, 1)
                        if (q, j) in turn_between:
                            turn_ln(ln, turn_between[q, j])
                for j in range(3, 8):
                    tile(0, j)
                if after_first is not None:
                    after_first()
                with pe.Fori(1, n // 4) as i:
                    for j in range(8):
                        tile(i, j)

            def rows_stage(ln, unit_base, tiles, seen, between=None):
                def ready(j, i=0):
                    pe.wait_ge(ht_low_ready, seen + j + 1 + 8 * i)

                for j in range(4):
                    pe.wait_ge(w_low_ready, 2 * unit_base + j + 1)
                    ready(j)
                    rows_half(unit_base, j, (ht_high[:, j, :], ht_low[:, j, :]), j == 0)
                if between is not None:
                    between()
                loops = (tiles - 8) // 8
                if loops > 1:
                    with pe.Fori(0, loops) as i:
                        for j in range(4, 12):
                            pe.wait_ge(w_low_ready, 2 * unit_base + 8 * i + j + 1)
                            ready(j, i)
                            rows_half(unit_base, j, (ht_high[:, j % 4, :], ht_low[:, j % 4, :]), False)
                for j in range(4 + (8 * loops if loops > 1 else 0), tiles - 4):
                    pe.wait_ge(w_low_ready, 2 * unit_base + j + 1)
                    ready(j)
                    rows_half(unit_base, j, (ht_high[:, j % 4, :], ht_low[:, j % 4, :]), False)
                if between is not None:
                    pe.wait_ge(spatial_add_ready, GM)
                rows_tail(ln, unit_base + tiles // 2 - 2, lambda j: (ht_high[:, j, :], ht_low[:, j, :]),
                          lambda j: ready(tiles - 4 + j))

            def row_sum_products():
                pe.wait_ge(ones_ready, 1)
                pe.wait_ge(ws_t_ready, 3)
                for b, bank in ((0, 3), (1, 0)):
                    nc.tensor.matmul(ps_m[:, bank, :], ones[:, :],
                                     ws_t[:, 4 * b:4 * b + 4, :].rearrange("p g c -> p (g c)"),
                                     start=True, stop=True).then_inc(row_sums, 1)

            def turn_small():
                pe.wait_ge(ws_masked, 1)
                for b in range(2):
                    turn(ps_y[:, b, :], ws_n[:, 4 * b:4 * b + 4, :].rearrange("p g c -> p (g c)")) \
                        .then_inc(ws_turned, 1)
                for s in rows_landed:
                    pe.wait_ge(s, 16)
                nc.tensor.transpose(ps_y[:, 2, 0:3 * GM], rows48[:, :], ident[0:3 * GM, 0:3 * GM]) \
                    .then_inc(ws_turned, 1)

            tall_stage(U_FA, N_FF, 0, 0, turn_small)
            pe.wait_ge(act_out, FM)
            pe.wait_ge(ws_t_ready, 3)
            rows_stage(1, U_FB, FM, 0, row_sum_products)
            turn_ln(1, 2)
            turn_ln(1, 3)
            for t in range(NT):
                for q in range(4):
                    if t == 0:
                        pe.wait_ge(w_low_ready, 2 * U_GV + q + 1)
                    pe.wait_ge(xt_low_ready, 2 * EVENTS + 4 * t + q + 1)
                    mm = wide_products((U_GV + q // 2) % SLOTS, q, t, ps_m[:, t, :])
                    if t == 1:
                        mm.then_inc(w_used, 1)
                    for e in {(0, 2): (4,), (0, 3): (5, 6), (1, 0): (7,)}.get((t, q), ()):
                        turn_ln(1, e)
            for j in range(4, 2 * N_GV):
                g, q = j // 4, j % 4
                if q == 0 and g >= 2:
                    pe.wait_ge(v_biased, NT * (g - 1))
                pe.wait_ge(w_low_ready, 2 * U_GV + j + 1)
                wide_half((U_GV + j // 2) % SLOTS, q, [ps_m[:, 2 * (g % 2) + t, :] for t in range(NT)]) \
                    .then_inc(w_used, 1)

            def mix_tile(m):
                pe.wait_ge(vn_ready, 2 * m + 2)
                if m >= 4:
                    pe.wait_ge(mixed_ready, m - 3)
                for t in range(NT):
                    mm = nc.tensor.matmul(ps_y[:, m % 4, t * P:(t + 1) * P], vn_tile[:, m % 2, t, :],
                                          ws_t[:, m // 2, :], start=True, stop=True)
                mm.then_inc(spatial_done, 1)

            mixed_after = {m: (m - 2,) for m in range(2, 10)}
            mixed_after.update({10: (8, 9), 11: (10,), 12: (11, 12), 13: (13,), 14: (14, 15)})
            for m in range(GM):
                pe.wait_ge(w_low_ready, 2 * U_GU + m + 1)
                if m in (0, 2):
                    pe.wait_ge(v_biased, (3 if m == 0 else 4) * NT)
                if m >= 4:
                    pe.wait_ge(act_out, FM + m - 3)
                tall_products((U_GU + m // 2) % SLOTS, m % 2, ps_m[:, m % 4, 0:SEQ]) \
                    .then_inc(w_used, 1)
                for n in mixed_after.get(m, ()):
                    mix_tile(n)
            pe.wait_ge(mixed_ready, GM)
            rows_stage(2, U_GO, GM, FM)

            tall_stage(U_FC, N_FF, FM + GM, 2)
            rows_stage(3, U_FD, FM, FM + GM)


_INS = ["x", "positions", "ln_gain", "ln_bias", "mix_w_in", "ret_gn_gain", "mix_w_out", "gmlp_w_uv",
        "gmlp_b_uv", "gmlp_ln_gain", "gmlp_ln_bias", "gmlp_w_s", "gmlp_b_s", "gmlp_w_out", "ffn_w_in",
        "ffn_w_out"]


def shape_constants():
    freq = (10000.0 ** (-np.arange(0, HD, 2) / HD)).astype(np.float32)
    gamma = 1.0 - 2.0 ** (-5.0 - np.arange(HEADS))
    diff = np.arange(SEQ)[None, None, :] - np.arange(P)[:, None, None]
    decay = np.where(diff >= 0, gamma[None, :, None] ** np.maximum(diff, 0), 0.0) * QK_SCALE
    return freq, decay.astype(np.float32).reshape(P, HEADS * SEQ)


def kernel(**inputs):
    import concourse.bacc as bacc
    from concourse.bass_utils import run_bass_kernel_spmd

    nc = bacc.Bacc("TRN2", target_bir_lowering=False, num_devices=1)
    arrays = {name: np.ascontiguousarray(inputs[name]) for name in _INS}
    arrays["inv_freq"], arrays["decay"] = shape_constants()
    args = [nc.dram_tensor(f"in_{name}", a.shape, mybir.dt.from_np(a.dtype), kind="ExternalInput").ap()
            for name, a in arrays.items()]
    args.append(nc.dram_tensor("out_0", (1, SEQ, D), F32, kind="ExternalOutput").ap())
    build(nc, *args)
    r = run_bass_kernel_spmd(nc, [{f"in_{name}": a for name, a in arrays.items()}], core_ids=[0])
    return r.results[0]["out_0"]
```
